# Optimizing a Trainium2 kernel written in Bass

```python
import jax, jax.numpy as jnp
from jax import lax
import numpy as np

D_MODEL = 2048
BATCH = 1
SEQ = 128
DEPTH = 2
DEC_BATCH = 1
DEC_SEQ = 256
PAST_LEN = 128

GRID_W = 64
N_MIXERS = 2
N_NA_LAYERS = (DEPTH + 1) // 2
N_DN_LAYERS = DEPTH // 2
EPS = 1e-6
Q_BLOCK = 128
NA_HEADS = 16
NA_HEAD_DIM = D_MODEL // NA_HEADS
NA_WIDTH = NA_HEADS * NA_HEAD_DIM
NA_IN = 4 * NA_WIDTH
WIN_R = 8
WIN_C = 16
DN_K_HEADS = 16
DN_V_HEADS = 32
DN_HEAD_DIM = 128
DN_KEY_WIDTH = DN_K_HEADS * DN_HEAD_DIM
DN_VAL_WIDTH = DN_V_HEADS * DN_HEAD_DIM
DN_CONV_WIDTH = 2 * DN_KEY_WIDTH + DN_VAL_WIDTH
DN_IN = DN_CONV_WIDTH + DN_VAL_WIDTH + 4 * DN_V_HEADS
DN_CONV = 5
DN_CHUNK = 64

kernel_name = "hybrid_natten_deltanet_diffusion_step"

def rmsnorm(x, w):
    xf = x.astype(jnp.float32)
    y = xf * lax.rsqrt(jnp.mean(xf * xf, axis=-1, keepdims=True) + EPS)
    return (y * w.astype(jnp.float32)).astype(x.dtype)

def l2norm(x):
    xf = x.astype(jnp.float32)
    return xf * lax.rsqrt(jnp.sum(xf * xf, axis=-1, keepdims=True) + EPS)

def ada_mod(cond, w, b):
    m = (jax.nn.silu(cond) @ w + b)[..., None, :]
    return jnp.split(m, 3, axis=-1)

def na_project(h, w_in):
    B, T, _ = h.shape
    q, k, v, z = jnp.split(h @ w_in, 4, axis=-1)
    shp = (B, T, NA_HEADS, NA_HEAD_DIM)
    return q.reshape(shp), k.reshape(shp), v.reshape(shp), z

def na_output(o, z, w_out):
    B, T = o.shape[:2]
    return (o.reshape(B, T, NA_WIDTH) * jax.nn.silu(z)) @ w_out

def context_attention(q, k, v):
    B, T, H, Dh = q.shape
    qb = jnp.moveaxis(q.reshape(B, T // Q_BLOCK, Q_BLOCK, H, Dh), 1, 0)

    def block(qi):
        s = jnp.einsum('bqhd,bkhd->bhqk', qi, k).astype(jnp.float32) * (Dh ** -0.5)
        p = jax.nn.softmax(s, axis=-1).astype(v.dtype)
        return jnp.einsum('bhqk,bkhd->bqhd', p, v)

    o = lax.map(block, qb)
    return jnp.moveaxis(o, 0, 1).reshape(B, T, H, Dh)

def neighbourhood_attention(q, k, v, ck, cv, rpb):
    B, T, H, Dh = q.shape
    rows = T // GRID_W
    wr = min(WIN_R, rows)
    qg = q.reshape(B, rows, GRID_W, H, Dh)
    kg = k.reshape(B, rows, GRID_W, H, Dh)
    vg = v.reshape(B, rows, GRID_W, H, Dh)
    cols = jnp.arange(GRID_W)
    col_start = jnp.clip(cols - WIN_C // 2, 0, GRID_W - WIN_C)
    col_in = (cols[None, :] >= col_start[:, None]) & (cols[None, :] < col_start[:, None] + WIN_C)
    dc_idx = jnp.clip(cols[None, :] - cols[:, None] + WIN_C - 1, 0, 2 * WIN_C - 2)
    scale = Dh ** -0.5
    n_loc = wr * GRID_W

    def row_block(r):
        rs = jnp.clip(r - wr // 2, 0, rows - wr)
        kb = lax.dynamic_slice_in_dim(kg, rs, wr, axis=1)
        vb = lax.dynamic_slice_in_dim(vg, rs, wr, axis=1)
        qr = lax.dynamic_index_in_dim(qg, r, axis=1, keepdims=False)
        s_loc = jnp.einsum('bqhd,bikhd->bhqik', qr, kb).astype(jnp.float32) * scale
        dr_idx = rs + jnp.arange(wr) - r + WIN_R - 1
        bias = rpb[:, dr_idx[None, :, None], dc_idx[:, None, :]]
        s_loc = jnp.where(col_in[:, None, :], s_loc + bias.astype(jnp.float32)[None], -jnp.inf)
        s_ctx = jnp.einsum('bqhd,bkhd->bhqk', qr, ck).astype(jnp.float32) * scale
        s = jnp.concatenate([s_loc.reshape(B, H, GRID_W, n_loc), s_ctx], axis=-1)
        p = jax.nn.softmax(s, axis=-1).astype(v.dtype)
        p_loc = p[..., :n_loc].reshape(B, H, GRID_W, wr, GRID_W)
        o = (jnp.einsum('bhqik,bikhd->bqhd', p_loc, vb)
             + jnp.einsum('bhqk,bkhd->bqhd', p[..., n_loc:], cv))
        return o

    out = lax.map(row_block, jnp.arange(rows))
    return jnp.moveaxis(out, 0, 1).reshape(B, T, H, Dh)

def short_conv(x, w):
    C = x.shape[-1]
    return lax.conv_general_dilated(
        x, w.astype(x.dtype)[:, None, :], window_strides=(1,),
        padding=[(DN_CONV // 2, DN_CONV // 2)],
        dimension_numbers=('NWC', 'WIO', 'NWC'), feature_group_count=C)

def chunk_gated_delta(q, k, v, g, beta, s0):
    B, H, T, Dk = k.shape
    Dv = v.shape[-1]
    n = T // DN_CHUNK

    def chunks(a):
        return a.astype(jnp.float32).reshape(B, H, n, DN_CHUNK, *a.shape[3:])

    q, k, v, g, beta = chunks(q), chunks(k), chunks(v), chunks(g), chunks(beta)
    gc = jnp.cumsum(g, axis=-1)
    idx = jnp.arange(DN_CHUNK)
    incl = idx[:, None] >= idx[None, :]
    strict = idx[:, None] > idx[None, :]
    decay = jnp.exp(jnp.where(incl, gc[..., :, None] - gc[..., None, :], -jnp.inf))
    kb = k * beta[..., None]
    a_mat = (jnp.where(strict, jnp.einsum('bhnid,bhnjd->bhnij', kb, k) * decay, 0.0)
             + jnp.eye(DN_CHUNK, dtype=jnp.float32))
    rhs = jnp.concatenate([v * beta[..., None], kb * jnp.exp(gc)[..., None]], axis=-1)
    sol = lax.linalg.triangular_solve(a_mat, rhs, left_side=True, lower=True, unit_diagonal=True)
    u, w = sol[..., :Dv], sol[..., Dv:]
    qk = jnp.einsum('bhnid,bhnjd->bhnij', q, k) * decay
    xs = tuple(jnp.moveaxis(a, 2, 0) for a in (q, k, u, w, qk, gc))

    def step(s, inp):
        q_i, k_i, u_i, w_i, qk_i, g_i = inp
        v_new = u_i - jnp.einsum('bhcd,bhde->bhce', w_i, s)
        o_i = (jnp.einsum('bhcd,bhde->bhce', q_i * jnp.exp(g_i)[..., None], s)
               + jnp.einsum('bhij,bhje->bhie', qk_i, v_new))
        g_last = g_i[..., -1:]
        s = (s * jnp.exp(g_last)[..., None]
             + jnp.einsum('bhcd,bhce->bhde', k_i * jnp.exp(g_last - g_i)[..., None], v_new))
        return s, o_i

    s, o = lax.scan(step, s0.astype(jnp.float32), xs)
    return jnp.moveaxis(o, 0, 2).reshape(B, H, T, Dv), s

def deltanet_mix(h, w_in, conv_w, a_log, dt_bias, norm_w, w_out, s0_fwd, s0_bwd):
    B, T, _ = h.shape
    proj = h @ w_in
    qkv = jax.nn.silu(short_conv(proj[..., :DN_CONV_WIDTH], conv_w))
    z = proj[..., DN_CONV_WIDTH:DN_CONV_WIDTH + DN_VAL_WIDTH]
    ba = proj[..., DN_CONV_WIDTH + DN_VAL_WIDTH:].reshape(B, T, 4, DN_V_HEADS).astype(jnp.float32)
    rep = DN_V_HEADS // DN_K_HEADS
    q = qkv[..., :DN_KEY_WIDTH].reshape(B, T, DN_K_HEADS, DN_HEAD_DIM)
    k = qkv[..., DN_KEY_WIDTH:2 * DN_KEY_WIDTH].reshape(B, T, DN_K_HEADS, DN_HEAD_DIM)
    v = qkv[..., 2 * DN_KEY_WIDTH:].reshape(B, T, DN_V_HEADS, DN_HEAD_DIM)
    q = jnp.repeat(l2norm(q) * (DN_HEAD_DIM ** -0.5), rep, axis=2)
    k = jnp.repeat(l2norm(k), rep, axis=2)
    beta = jax.nn.sigmoid(ba[:, :, 0:2])
    g = -jnp.exp(a_log.astype(jnp.float32)) * jax.nn.softplus(ba[:, :, 2:4] + dt_bias.astype(jnp.float32))
    qh = jnp.transpose(q, (0, 2, 1, 3))
    kh = jnp.transpose(k, (0, 2, 1, 3))
    vh = jnp.transpose(v, (0, 2, 1, 3))
    gh = jnp.transpose(g, (0, 2, 3, 1))
    bh = jnp.transpose(beta, (0, 2, 3, 1))

    def rev(a):
        return jnp.flip(a, axis=2)

    o_f, s_f = chunk_gated_delta(qh, kh, vh, gh[:, 0], bh[:, 0], s0_fwd)
    o_b, s_b = chunk_gated_delta(rev(qh), rev(kh), rev(vh), rev(gh[:, 1]), rev(bh[:, 1]), s0_bwd)
    o = jnp.transpose(o_f + rev(o_b), (0, 2, 1, 3))
    o = rmsnorm(o, norm_w) * jax.nn.silu(z.reshape(B, T, DN_V_HEADS, DN_HEAD_DIM).astype(jnp.float32))
    out = o.reshape(B, T, DN_VAL_WIDTH).astype(h.dtype) @ w_out
    return out, jnp.stack([s_f, s_b], axis=1)

def context_trunk(x, c_ctx, norm_w, ada_w, ada_b, na_w_in, na_w_out,
                  dn_w_in, dn_conv_w, dn_a_log, dn_dt_bias, dn_norm_w, dn_w_out, final_norm_w):
    B = x.shape[0]
    ks, vs, ss = [], [], []
    for i in range(DEPTH):
        shift, scale, gate = ada_mod(c_ctx, ada_w[i], ada_b[i])
        h = rmsnorm(x, norm_w[i]) * (1 + scale) + shift
        j = i // N_MIXERS
        if i % N_MIXERS == 0:
            q, k, v, z = na_project(h, na_w_in[j])
            out = na_output(context_attention(q, k, v), z, na_w_out[j])
            ks.append(k)
            vs.append(v)
        else:
            zeros = jnp.zeros((B, DN_V_HEADS, DN_HEAD_DIM, DN_HEAD_DIM), jnp.float32)
            out, s = deltanet_mix(h, dn_w_in[j], dn_conv_w[j], dn_a_log[j], dn_dt_bias[j],
                                  dn_norm_w[j], dn_w_out[j], zeros, zeros)
            ss.append(s.astype(x.dtype))
        x = x + gate * out
    return rmsnorm(x, final_norm_w), jnp.stack(ks, axis=1), jnp.stack(vs, axis=1), jnp.stack(ss, axis=1)

def latent_trunk(x, c, cache_na_k, cache_na_v, state_dn, norm_w, ada_w, ada_b, na_w_in, na_w_out,
                 na_rpb, dn_w_in, dn_conv_w, dn_a_log, dn_dt_bias, dn_norm_w, dn_w_out, final_norm_w):
    for i in range(DEPTH):
        shift, scale, gate = ada_mod(c, ada_w[i], ada_b[i])
        h = rmsnorm(x, norm_w[i]) * (1 + scale) + shift
        j = i // N_MIXERS
        if i % N_MIXERS == 0:
            q, k, v, z = na_project(h, na_w_in[j])
            o = neighbourhood_attention(q, k, v, cache_na_k[:, j], cache_na_v[:, j], na_rpb[j])
            out = na_output(o, z, na_w_out[j])
        else:
            out, _ = deltanet_mix(h, dn_w_in[j], dn_conv_w[j], dn_a_log[j], dn_dt_bias[j],
                                  dn_norm_w[j], dn_w_out[j], state_dn[:, j, 0], state_dn[:, j, 1])
        x = x + gate * out
    return rmsnorm(x, final_norm_w)

def setup_inputs(seed: int = 0) -> dict:
    key = jax.random.key(seed)
    ks = jax.random.split(key, 24)
    f32 = jnp.float32

    def nrm(k, shape, s=1.0):
        return jax.random.normal(k, shape, f32) * s

    dt = jnp.exp(jax.random.uniform(ks[19], (N_DN_LAYERS, 2, DN_V_HEADS), f32,
                                    jnp.log(1e-3), jnp.log(1e-1)))
    return {
        "x_prompt": nrm(ks[0], (BATCH, SEQ, D_MODEL)),
        "x_sample": nrm(ks[1], (DEC_BATCH, DEC_SEQ, D_MODEL)),
        "cache_na_k": nrm(ks[2], (DEC_BATCH, N_NA_LAYERS, PAST_LEN, NA_HEADS, NA_HEAD_DIM)),
        "cache_na_v": nrm(ks[3], (DEC_BATCH, N_NA_LAYERS, PAST_LEN, NA_HEADS, NA_HEAD_DIM)),
        "state_dn": nrm(ks[4], (DEC_BATCH, N_DN_LAYERS, 2, DN_V_HEADS, DN_HEAD_DIM, DN_HEAD_DIM), 0.1),
        "c": nrm(ks[5], (DEC_BATCH, D_MODEL)),
        "c_ctx": nrm(ks[6], (D_MODEL,)),
        "norm_w": 1.0 + nrm(ks[7], (DEPTH, D_MODEL), 0.02),
        "ada_w": nrm(ks[8], (DEPTH, D_MODEL, 3 * D_MODEL), 0.5 * D_MODEL ** -0.5),
        "ada_b": nrm(ks[9], (DEPTH, 3 * D_MODEL), 0.02),
        "na_w_in": nrm(ks[10], (N_NA_LAYERS, D_MODEL, NA_IN), D_MODEL ** -0.5),
        "na_w_out": nrm(ks[11], (N_NA_LAYERS, NA_WIDTH, D_MODEL), NA_WIDTH ** -0.5),
        "na_rpb": nrm(ks[12], (N_NA_LAYERS, NA_HEADS, 2 * WIN_R - 1, 2 * WIN_C - 1), 0.1),
        "dn_w_in": nrm(ks[13], (N_DN_LAYERS, D_MODEL, DN_IN), D_MODEL ** -0.5),
        "dn_conv_w": nrm(ks[14], (N_DN_LAYERS, DN_CONV, DN_CONV_WIDTH), DN_CONV ** -0.5),
        "dn_a_log": jnp.log(jax.random.uniform(ks[15], (N_DN_LAYERS, 2, DN_V_HEADS), f32, 1.0, 16.0)),
        "dn_dt_bias": jnp.log(jnp.expm1(dt)),
        "dn_norm_w": 1.0 + nrm(ks[16], (N_DN_LAYERS, DN_HEAD_DIM), 0.02),
        "dn_w_out": nrm(ks[17], (N_DN_LAYERS, DN_VAL_WIDTH, D_MODEL), DN_VAL_WIDTH ** -0.5),
        "final_norm_w": 1.0 + nrm(ks[18], (D_MODEL,), 0.02),
    }

def reference(x_prompt, x_sample, cache_na_k, cache_na_v, state_dn, c, c_ctx, norm_w, ada_w, ada_b,
              na_w_in, na_w_out, na_rpb, dn_w_in, dn_conv_w, dn_a_log, dn_dt_bias, dn_norm_w,
              dn_w_out, final_norm_w):
    y_prompt, new_na_k, new_na_v, new_state_dn = context_trunk(
        x_prompt, c_ctx, norm_w, ada_w, ada_b, na_w_in, na_w_out,
        dn_w_in, dn_conv_w, dn_a_log, dn_dt_bias, dn_norm_w, dn_w_out, final_norm_w)
    y_sample = latent_trunk(
        x_sample, c, cache_na_k, cache_na_v, state_dn, norm_w, ada_w, ada_b, na_w_in, na_w_out,
        na_rpb, dn_w_in, dn_conv_w, dn_a_log, dn_dt_bias, dn_norm_w, dn_w_out, final_norm_w)
    return (y_prompt, y_sample, new_na_k, new_na_v, new_state_dn)


_drawn_inputs = setup_inputs


def setup_inputs(seed=0):
    import zlib

    import numpy as np

    out = dict(_drawn_inputs(seed))
    spreads = {}
    factors = {'cache_na_k': 3.45,
     'cache_na_v': 2.822,
     'na_rpb': 64.0,
     'dn_norm_w': 27.072,
     'final_norm_w': 7.833}
    for name, (base, spread) in spreads.items():
        noise = np.random.default_rng([zlib.crc32(name.encode()), seed]).standard_normal(out[name].shape)
        drawn = base * np.exp(spread * noise) if base else spread * noise
        out[name] = __import__('jax').numpy.asarray(drawn.astype(out[name].dtype))
    for name, factor in factors.items():
        out[name] = (out[name] * factor).astype(out[name].dtype)
    return out
```

```python
from contextlib import ExitStack

import concourse.bass as bass
import numpy as np
from concourse import mybir

F32 = mybir.dt.float32
F32R = mybir.dt.float32r
ACT = mybir.ActivationFunctionType
ALU = mybir.AluOpType
AX_X = mybir.AxisListType.X

P = 128
D_MODEL = 2048
KT = D_MODEL // P
CTX = 128
LAT = 256
T = CTX + LAT
CHUNKS = T // P
ROWS, GRID_W = 4, 64
WIN_R, WIN_C = 8, 16
BIAS_W = 2 * GRID_W - 1
NA_HEADS = 16
DN_K_HEADS = 16
DN_V_HEADS = 32
HALF_K = KT // 2
HALF = HALF_K * P
RAW_SLOTS = 4
SPLIT_SLOTS = 4
LOOKAHEAD = 3
CONV = 5
PAD = CONV // 2
LAT_AT = CTX + 2 * PAD
PADDED = T + 3 * PAD
CONV_OUT = PADDED - 2 * PAD
EPS = 1e-6
MASKED = -1e30
SCALE = float(P) ** -0.5
GROUP = 8
CREDIT = 1000
SMALL_LOADS = 10 + ROWS * ROWS
FILL = 8

CONSTS = ["ident", "ones", "lt", "gt", "le", "ge", "near", "grid"]


def shape_constants():
    m, i = np.arange(P)[:, None], np.arange(P)[None, :]
    grid = np.zeros((P, P), np.float32)
    col, key = np.arange(P)[:, None] % GRID_W, np.arange(GRID_W)[None, :]
    first = np.clip(col - WIN_C // 2, 0, GRID_W - WIN_C)
    grid[:, :GRID_W] = np.where((key >= first) & (key < first + WIN_C), 0.0, MASKED)
    tables = {"ident": m == i, "ones": m >= 0, "le": m <= i, "ge": m >= i, "gt": m > i, "lt": m < i,
              "near": m // 16 == i // 16, "grid": grid}
    return np.concatenate([np.broadcast_to(tables[n], (P, P)).astype(np.float32) for n in CONSTS], axis=1)


class Steps:

    def __init__(self, known=None):
        self.known, self.order, self.turns, self.phase = known, {}, {}, None
        self.sems = {}

    def enter(self, phase, turns):
        self.phase, self.turns[phase] = phase, turns

    def done(self, engine, name, instruction):
        self.order.setdefault((self.phase, engine), []).append(name)
        return instruction.then_inc(self.sems[engine], 1)

    def base(self, engine, phase):
        total = CREDIT
        for p, turns in self.known.turns.items():
            if p == phase:
                break
            total += turns * len(self.known.order.get((p, engine), []))
        return total

    def per_turn(self, engine):
        return len(self.known.order.get((self.phase, engine), [])) if self.known else 0

    def count(self, engine, name):
        if self.known is None:
            return CREDIT
        if name not in self.known.order.get((self.phase, engine), []):
            return None
        return self.base(engine, self.phase) + self.known.order[self.phase, engine].index(name) + 1



def plan_fill(items, halves):
    parts = [("part", k, f) for k in halves for f in range(FILL)]
    plan, used = [], 0
    for n, item in enumerate(items):
        want = (n + 1) * len(parts) // (len(items) + 1)
        plan += parts[used:want] + [item]
        used = want
    return plan + parts[used:]


def with_ada(halves):
    plan = []
    for k in halves:
        plan += plan_fill([], [k]) + [("ada", k)]
    return plan


NA_PLAN = (with_ada([0, 1, 2, 3, 4]) + [("scores",)] + with_ada([5, 6]) + [("values",)] + plan_fill([], [7])
           + [("turn_probs",), ("ada", 7), ("attend",)])

NEWTON = 3
INVERT = [["ct"], ["p2", "p2t"], ["p4", "p4t", "x1"], ["p8t", "x2"], ["x3"], ["xt0"]]
for _n in range(1, NEWTON + 1):
    INVERT += [[f"t{_n}"], [f"xn{_n}", f"xt{_n}"]]
INVERT += [["res"], ["xf"]]
READ_BY_SCALAR = {"p2", "p2t", "p4", "p4t", "p8t", "xt0"} | {f"x{a}{n}" for a in "nt" for n in range(1, NEWTON + 1)}

_chain = [(5, ("norms",)), (2, ("decay", 0)), (2, ("decay", 1)), (2, ("broad", 1)), (0, ("unit",)), (2, ("decay", 2)),
          (2, ("broad", 2)), (1, ("gram", 0)), (2, ("gram", 1)), (2, ("gram", 2)), (1, ("values", 0)),
          (1, ("values", 1))]
for _stage in range(len(INVERT) - 1):
    _chain += [(3 if _stage < 2 and c == 0 else 2 if _stage < 2 else 1, ("invert", _stage, c)) for c in range(CHUNKS)]
_chain += [(1, ("recall", "A"))] + [(1, ("invert", len(INVERT) - 1, c)) for c in range(CHUNKS)]
_chain += [(3, ("apply", "0")), (0, ("apply", "A")), (3, ("state", "A")), (0, ("state", "0")), (3, ("recall", "B")),
           (3, ("apply", "B")), (3, ("out",)), (0, ("squares",)), (3, ("out_norm",))]


def merge(chain, parts):
    total = sum(weight for weight, _ in chain)
    plan, seen, used = [], 0, 0
    for weight, item in chain:
        seen += weight
        want = seen * len(parts) // (total + 2)
        plan += parts[used:want] + [item]
        used = want
    return plan + parts[used:]


TAPS_AT = 4 * FILL
DN_PARTS = [("part", k, f) for k in range(12) for f in range(FILL)]
DN_CHAIN = [item for _, item in _chain]
DN_PLAN = merge(_chain, DN_PARTS)
DN_PLANS = {"dnP": DN_PARTS + [("squares",), ("gates",)], "dn0": DN_PLAN + [("gates",)], "dn1": DN_PLAN + [("gates",)],
            "dnE": DN_CHAIN}


INVERT_OPERANDS = {"p2": ("e", "d"), "p2t": ("d", "e"), "p4": ("g", "f"), "p4t": ("f", "g"), "x1": ("g", "x"),
                   "p8t": ("d", "e"), "x2": ("e", "x"), "x3": ("f", "x"), "t": ("mtr", "x"), "xn": ("g", "d"),
                   "xt": ("d", "g"), "xf": ("g", "d")}
INVERT_NEEDS = {"ct": [("dve", "c")], "p2": [("pool", "near"), ("dve", "near")], "p2t": [],
                "p4": [("act", "p2t_")], "p4t": [], "x1": [("pool", "x0")],
                "p8t": [("act", "p4t_")], "x2": [("dve", "x1_")], "x3": [("act", "p8t_"), ("dve", "x2_")],
                "xt0": [("dve", "x3_")], "res": [("act", f"xt{NEWTON}_")], "xf": [("dve", "res_")]}
for _n in range(1, NEWTON + 1):
    INVERT_NEEDS |= {f"t{_n}": [("act", f"xt{_n - 1}_"), ("act", "mtr")], f"xn{_n}": [("dve", f"t{_n}_")],
                     f"xt{_n}": []}


def dn_products():
    made = []
    for item in DN_CHAIN:
        what, arg = item[0], item[1] if len(item) > 1 else None
        if what == "decay":
            made.append((f"decay{arg}", "act"))
        elif what == "broad":
            made.append((f"broad{arg}", "act"))
        elif what == "norms":
            made += [("ss0", "act"), ("ss1", "act")]
        elif what == "gram":
            made.append((f"gram{arg}", "act"))
        elif what == "values":
            made.append((f"values{arg}", "act"))
        elif what == "invert":
            made += [(f"{p}_{item[2]}", "act" if p in READ_BY_SCALAR else "dve") for p in INVERT[arg]]
        elif what in ("recall", "apply"):
            made.append((f"{what}{arg}", "act" if what == "apply" and arg == "B" else "dve"))
        elif what == "state":
            made.append((f"state{arg}", "act" if arg == "0" else "dve"))
        elif what == "out_norm":
            made += [("on0", "act"), ("on1", "act")]
    return made


PRODUCTS = dn_products()
PRODUCT_AT = {name: n for n, (name, _) in enumerate(PRODUCTS)}
RING, RING_AT = 4, 2
assert len(PRODUCTS) % RING == 0
SCAN = {"0": (0, 0), "A": (1, 2), "B": (2, 1)}


def emit(nc, known, dram):
    steps = Steps(known)
    done = steps.done

    with ExitStack() as ctx:
        def sb(name, shape, dt=F32):
            return ctx.enter_context(nc.sbuf_tensor(name, shape, dt))

        def sem(name):
            return ctx.enter_context(nc.semaphore(name))

        banks = [ctx.enter_context(nc.psum_tensor(f"bank{n}", [P, 512], F32)) for n in range(8)]

        raw = sb("raw", [P, RAW_SLOTS, HALF])
        w_hi = sb("w_hi", [P, SPLIT_SLOTS, HALF], F32R)
        w_lo = sb("w_lo", [P, SPLIT_SLOTS, HALF], F32R)
        h_hi = sb("h_hi", [P, KT, T], F32R)
        h_lo = sb("h_lo", [P, KT, T], F32R)
        y = sb("y", [P, KT + 2, T])
        consts = sb("consts", [P, len(CONSTS), P])
        K = {n: consts[:, j, :] for j, n in enumerate(CONSTS)}
        mods = sb("mods", [P, 2 * 3 * KT, 2])
        ada_b = sb("ada_b", [P, 2 * 3 * KT])
        cond = sb("cond", [P, KT, 2])
        norm_w = sb("norm_w", [P, 3, KT])
        gain = sb("gain", [P, KT, 2])
        bias_eps = sb("bias_eps", [P, 2])
        twice = sb("twice", [P, P])
        conv_w = sb("conv_w", [P, DN_K_HEADS, 4, CONV])
        alog_dt = sb("alog_dt", [P, 3])
        dn_norm_w = sb("dn_norm_w", [P, 1])
        TAB = [P, CHUNKS, 2, DN_V_HEADS]
        neg_egc = sb("neg_egc", TAB)
        beta_egl = sb("beta_egl", TAB)
        egl = sb("egl", TAB)
        bg = sb("bg", [P, CHUNKS, P])
        beta_now = sb("beta_now", [P, CHUNKS, 2, 2])
        g_now = sb("g_now", [P, CHUNKS, 2, 2])

        scratch_at = (nc.sbuf_base + 63) // 64 * 64
        scratch_end = nc.sbuf_usable_end

        class Region:
            def __init__(self, at=0):
                self.at = scratch_at + at

            def take(self, name, shape, dt=F32):
                size = 4 * int(np.prod(shape[1:]))
                t = nc.alloc_sbuf_tensor_at(name, shape, dt, offset=self.at)
                self.at += (size + 31) // 32 * 32
                assert self.at <= scratch_end, (name, self.at - scratch_end)
                return t

        region = Region()
        x = y[:, 2:KT + 2, :]
        y_hi = region.take("y_hi", [P, KT, T], F32R)
        y_lo = region.take("y_lo", [P, KT, T], F32R)
        rstd = region.take("rstd", [P, T])
        logs = region.take("logs", [P, T])
        squares = region.take("squares", [P, 2, T])
        scaled = region.take("scaled", [P, 2, T])
        shifted = region.take("shifted", [P, 2, T])
        region = Region()
        bias = region.take("bias", [P, 2, NA_HEADS, ROWS * GRID_W])
        cache_k = region.take("cache_k", [P, NA_HEADS, P])
        cache_v = region.take("cache_v", [P, NA_HEADS, P])
        qk = region.take("qk", [P, 2, T])
        vT = region.take("vT", [P, T])
        V = region.take("V", [P, CHUNKS, P])
        gate_na = region.take("gate_na", [P, T])
        cache_k1 = region.take("cache_k1", [P, P])
        cache_v1 = region.take("cache_v1", [P, P])
        probs = region.take("probs", [P, CTX + 2 * T])
        raw_ada = region.take("raw_ada", [P, 2, HALF])
        probsT = region.take("probsT", [P, CTX + CHUNKS * LAT])
        stats = region.take("stats", [P, 3, 3])
        region = Region()
        inv = {}
        f32r_at = region.at
        for c in range(CHUNKS):
            for name in ("d", "e", "f", "g", "x"):
                inv[name, c] = region.take(f"inv_{name}{c}", [P, 4, P], F32R)
        overlay = Region(f32r_at - scratch_at)
        vn = {s: overlay.take(f"v_new{s}", [P, 4, P]) for s in "0AB"}
        vs = {s: overlay.take(f"v_state{s}", [P, 4, P]) for s in "0A"}
        s_out = overlay.take("s_out", [P, 4, P])
        o_sq = overlay.take("o_sq", [P, 2, T])
        o_rs = overlay.take("o_rs", [P, 2, T])
        o_n = overlay.take("o_n", [P, 2, T])
        qk_sq = overlay.take("qk_sq", [P, 2, CONV_OUT])
        qk_rs = overlay.take("qk_rs", [P, 2, CONV_OUT])
        assert overlay.at <= region.at
        for c in range(CHUNKS):
            inv["mtr", c] = Region(region.at - scratch_at).take(f"inv_mtr{c}", [P, 4, P], F32R)
            for name in ("c", "mt"):
                inv[name, c] = region.take(f"inv_{name}{c}", [P, 4, P])
        R = {"A": inv["mt", 1], "B": inv["mt", 2]}
        dn_qk = region.take("dn_qk", [P, 2, T])
        padded = region.take("padded", [P, 2, PADDED])
        dn_v = region.take("dn_v", [P, CHUNKS, 2, P])
        k_nat = region.take("k_nat", [P, CHUNKS, P])
        gram = region.take("gram", [P, 2, 2, P])
        decay = [region.take(f"decay{c}", [P, 4, P]) for c in range(CHUNKS)]
        q_dec = [None] + [region.take(f"q_dec{c}", [P, 4, P]) for c in (1, 2)]
        S = region.take("S", [P, 4, P])
        conv = region.take("conv", [P, 4, CONV_OUT])
        g_mask = [inv["c", c] for c in range(CHUNKS)]
        overlay = Region(f32r_at - scratch_at)
        bgT = overlay.take("bgT", [P, T])
        bt = overlay.take("bt", [P, T])
        bt2 = overlay.take("bt2", [P, T])

        s = {n: sem(n) for n in ("tensor_steps", "scalar_steps", "vector_steps", "pool_steps", "hi_ready",
                                 "halves_done", "evacuated", "small_in", "x_in", "x_out", "bias_in", "k_out",
                                 "pool_waits", "v_out", "state_in", "state_out", "y_out")}
        steps.sems = {"pe": s["tensor_steps"], "act": s["scalar_steps"], "dve": s["vector_steps"],
                      "pool": s["pool_steps"]}
        ada_full = [sem(f"ada_full{n}") for n in range(2)]
        ada_used = sem("ada_used")
        raw_full = [sem(f"raw_full{n}") for n in range(RAW_SLOTS)]
        consumed = [sem(f"consumed{n}") for n in range(RAW_SLOTS)]

        pos = {}
        n0 = m0 = t0 = 0
        for phase, turns, split, plain in (("ada", 4, 0, 16), ("na", NA_HEADS, 8, 0), ("out0", KT // 2, 4, 0),
                                           ("ba", 1, 2, 0), ("dnP", 1, 12, 0), ("dn0", GROUP, 12, 0),
                                           ("outA", KT // 2, 4, 0), ("dn1", GROUP - 1, 12, 0), ("outB", KT // 2, 4, 0)):
            pos[phase] = (n0, m0, split + plain, split, t0, split // 2)
            n0, m0, t0 = n0 + turns * (split + plain), m0 + turns * split, t0 + turns * split // 2
        N_HALVES = n0
        assert N_HALVES == dram["stream"].shape[0], (N_HALVES, dram["stream"].shape)

        def raw_wait(eng, phase, turn, k):
            n, _, per, _, _, _ = pos[phase]
            eng.wait_ge(raw_full[(n + k) % RAW_SLOTS], 16 * ((n + k) // RAW_SLOTS + 1) + turn * (16 * per // RAW_SLOTS))
            return (n + k) % RAW_SLOTS

        def split_place(phase, turn, k):
            n, m, per, split, _, _ = pos[phase]
            ahead, kk = divmod(k, split)
            if phase == "ba":
                ahead, kk = 0, k
            raw_n = n + ahead * per + kk
            return raw_n, m + k

        def split_hi(act, phase, turn, k):
            raw_n, mk = split_place(phase, turn, k)
            _, _, per, split, _, _ = pos[phase]
            act.wait_ge(raw_full[raw_n % RAW_SLOTS], 16 * (raw_n // RAW_SLOTS + 1) + turn * (16 * per // RAW_SLOTS))
            if mk >= SPLIT_SLOTS:
                act.wait_ge(s["halves_done"], mk - SPLIT_SLOTS + 1 + turn * split)
            nc.scalar.activation(w_hi[:, mk % SPLIT_SLOTS, :], raw[:, raw_n % RAW_SLOTS, :], ACT.Copy)\
                .then_inc(s["hi_ready"], 1)

        def split_lo(dve, phase, turn, k):
            raw_n, mk = split_place(phase, turn, k)
            split = pos[phase][3]
            dve.wait_ge(s["hi_ready"], mk + 1 + turn * split)
            nc.vector.tensor_tensor(w_lo[:, mk % SPLIT_SLOTS, :], raw[:, raw_n % RAW_SLOTS, :],
                                    w_hi[:, mk % SPLIT_SLOTS, :].bitcast(F32), ALU.subtract)\
                .then_inc(consumed[raw_n % RAW_SLOTS], 1)

        def multiply(pe, phase, turn, k, part, hi, lo):
            raw_n, mk = split_place(phase, turn, k)
            _, m, per, split, t, tiles = pos[phase]
            tile, half = k // 2, k % 2
            bank = banks[(t + tile) % 2]
            if part == 0:
                pe.wait_ge(consumed[raw_n % RAW_SLOTS], raw_n // RAW_SLOTS + 2 + turn * (per // RAW_SLOTS))
                if half == 0 and t + tile >= 2:
                    pe.wait_ge(s["evacuated"], t + tile - 1 + turn * tiles)
            each = HALF_K // FILL
            for j in range(part * each, (part + 1) * each):
                kt = half * HALF_K + j
                w = slice(j * P, (j + 1) * P)
                slot = mk % SPLIT_SLOTS
                nc.tensor.matmul(bank[:, 0:T], w_hi[:, slot, w], hi[:, kt, :], start=kt == 0, stop=False)
                nc.tensor.matmul(bank[:, 0:T], w_hi[:, slot, w], lo[:, kt, :], start=False, stop=False)
                last = nc.tensor.matmul(bank[:, 0:T], w_lo[:, slot, w], hi[:, kt, :], start=False, stop=kt == KT - 1)
            if part == FILL - 1:
                last.then_inc(s["halves_done"], 1)

        def tile_done(eng, phase, turn, tile):
            _, m, _, split, t, _ = pos[phase]
            eng.wait_ge(s["halves_done"], m + 2 * tile + 2 + turn * split)
            return banks[(t + tile) % 2]

        def tile_read(eng, phase, turn, tile):
            _, _, _, _, t, tiles = pos[phase]
            eng.wait_ge(s["evacuated"], t + tile + 1 + turn * tiles)

        def y_row(n):
            return y[:, bass.ds(n, 1), :].rearrange("p a t -> p (a t)")

        def half_used(eng, phase, turn, k):
            n, _, per, _, _, _ = pos[phase]
            eng.wait_ge(consumed[(n + k) % RAW_SLOTS], (n + k) // RAW_SLOTS + 2 + turn * (per // RAW_SLOTS))

        def heads(phase, turn):
            if phase == "dnP":
                return None, 0, None, KT
            if phase == "dn0":
                return turn, turn + 1, turn * -2 + KT, turn * -2 + (KT - 2)
            if phase == "dn1":
                return turn + GROUP, turn + (GROUP + 1), turn * 2, turn * 2 + 2
            return 2 * GROUP - 1, None, KT - 2, None

        def barrier(eng, me, phase):
            names = [p for p, _ in PHASES]
            tiles = sum(turns * pos[p][5] for p, turns in PHASES[:names.index(phase)] if p in pos)
            if tiles:
                eng.wait_ge(s["evacuated"], tiles)
            for other in ("pe", "act", "dve", "pool"):
                if known is not None:
                    eng.wait_ge(steps.sems[other], steps.base(other, phase))

        def ring(name):
            return banks[RING_AT + PRODUCT_AT[name] % RING]

        def ring_free(name):
            n = PRODUCT_AT[name] - RING
            before, reader = PRODUCTS[n]
            return reader, "v_newB" if before == "applyB" else before, n < 0

        def wait_steps(eng, turn, *which):
            latest = {}
            for engine, name, *back in which:
                at = steps.count(engine, name)
                if at is None:
                    continue
                at -= steps.per_turn(engine) if back and back[0] else 0
                latest[engine] = max(at, latest.get(engine, 0))
            for engine, at in latest.items():
                eng.wait_ge(steps.sems[engine], at + turn * steps.per_turn(engine) if steps.known else CREDIT)

        PHASES = [("start", 1), ("ada", 4), ("mod0", 1), ("na", NA_HEADS), ("ysplit0", 1), ("fetch0", 1), ("out0", KT // 2),
                  ("norm1", 1), ("mod1", 1), ("ba", 1), ("keep0", 1), ("dnP", 1), ("dn0", GROUP),
                  ("ysplitA", 1), ("fetchA", 1), ("outA", KT // 2), ("keep1", 1), ("dn1", GROUP - 1), ("dnE", 1), ("ysplitB", 1),
                  ("fetchB", 1), ("outB", KT // 2), ("norm2", 1), ("final", 1)]

        def run(eng, me, parts):
            for phase, turns in PHASES:
                steps.enter(phase, turns)
                barrier(eng, me, phase)
                body = parts.get(phase)
                if body is None:
                    continue
                if turns == 1:
                    body(eng, phase, 0)
                elif phase == "outB":
                    with eng.Fori(0, turns - 1) as turn:
                        body(eng, phase, turn)
                    body(eng, phase, turns - 1, last=True)
                else:
                    with eng.Fori(0, turns) as turn:
                        body(eng, phase, turn)

        block = ctx.enter_context(nc.Block())

        @block.sync
        def _(sp):
            def load(n, slot, turn):
                sp.wait_ge(consumed[slot], turn + 1)
                sp.dma_start(raw[:, slot, :], dram["stream"][bass.ds(n, 1)].rearrange("a p f -> p (a f)"))\
                    .then_inc(raw_full[slot], 16)

            with sp.Fori(0, N_HALVES // RAW_SLOTS) as turn:
                for slot in range(RAW_SLOTS):
                    load(RAW_SLOTS * turn + slot, slot, turn)
            for slot in range(N_HALVES % RAW_SLOTS):
                load(N_HALVES // RAW_SLOTS * RAW_SLOTS + slot, slot, N_HALVES // RAW_SLOTS)

        @block.tensor
        def _(pe):
            pe.sem_inc(s["tensor_steps"], CREDIT)
            pe.sem_inc(ada_used, 2)

            def sum_squares(pe, phase, turn):
                for k in range(KT):
                    wait_steps(pe, turn, ("act", f"square{k}"))
                    mm = nc.tensor.matmul(banks[2][:, 0:T], K["ones"], squares[:, k % 2, :], start=k == 0,
                                          stop=k == KT - 1)
                    done("pe", f"squared{k}", mm)

            def start(pe, phase, turn):
                pe.wait_ge(s["small_in"], 16 * SMALL_LOADS)
                sum_squares(pe, phase, turn)

            def ada_half(bank, weights, k):
                tile, half = k // 2, k % 2
                for j in range(HALF_K):
                    kt = half * HALF_K + j
                    mm = nc.tensor.matmul(bank[:, 2 * tile:2 * tile + 2], weights[:, j * P:(j + 1) * P],
                                          cond[:, kt, :], start=kt == 0, stop=kt == KT - 1)
                return mm

            def ada(pe, phase, turn):
                for g in range(2):
                    wait_steps(pe, turn, ("dve", f"mods{g}", 1))
                    for k in range(8):
                        slot = raw_wait(pe, phase, turn, 8 * g + k)
                        ada_half(banks[4 + g], raw[:, slot, :], k).then_inc(consumed[slot], 1)

            def na(pe, phase, turn):
                for item in NA_PLAN:
                    if item[0] == "part":
                        multiply(pe, phase, turn, item[1], item[2], h_hi, h_lo)
                    elif item[0] == "scores":
                        tile_read(pe, phase, turn, 1)
                        wait_steps(pe, turn, ("dve", "y", 1), ("pool", "cache_k1"))
                        mm = nc.tensor.matmul(banks[2][:, 0:CTX], qk[:, 0, 0:CTX], qk[:, 1, 0:CTX], start=True, stop=True)
                        done("pe", "scores0", mm)
                        for r in range(2):
                            q = qk[:, 0, CTX + r * P:CTX + (r + 1) * P]
                            nc.tensor.matmul(banks[3 + r][:, 0:LAT], q, qk[:, 1, CTX:T], start=True, stop=True)
                            mm = nc.tensor.matmul(banks[3 + r][:, LAT:T], q, cache_k1[:], start=True, stop=True)
                            done("pe", f"scores{r + 1}", mm)
                    elif item[0] == "values":
                        tile_read(pe, phase, turn, 2)
                        wait_steps(pe, turn, ("act", "V", 1))
                        for c in range(CHUNKS):
                            mm = nc.tensor.transpose(banks[5][:, c * P:(c + 1) * P], vT[:, c * P:(c + 1) * P], K["ident"])
                        done("pe", "values", mm)
                    elif item[0] == "turn_probs":
                        wait_steps(pe, turn, ("pool", "probs2"), ("dve", "probsT0", 1))
                        nc.tensor.transpose(banks[6][:, 0:P], probs[:, 0:P], K["ident"])

                        def turned(bank, at, c):
                            for r in range(2):
                                src = probs[:, CTX + r * T + c * P:CTX + r * T + (c + 1) * P]
                                mm = nc.tensor.transpose(bank[:, at + r * P:at + (r + 1) * P], src, K["ident"])
                            return mm
                        done("pe", "probsT0", turned(banks[6], P, 0))
                        turned(banks[2], 0, 1)
                        done("pe", "probsT1", turned(banks[2], LAT, 2))
                    elif item[0] == "attend":
                        wait_steps(pe, turn, ("dve", "probsT1"), ("act", "V"), ("pool", "cache_v1"))
                        nc.tensor.matmul(banks[3][:, 0:CTX], V[:, 0, :], probsT[:, 0:CTX], start=True, stop=True)
                        for c, values in enumerate((V[:, 1, :], V[:, 2, :], cache_v1[:])):
                            mm = nc.tensor.matmul(banks[3][:, CTX:T], values,
                                                  probsT[:, CTX + c * LAT:CTX + (c + 1) * LAT], start=c == 0,
                                                  stop=c == 2)
                        done("pe", "attend", mm)
                    else:
                        k = item[1]
                        if k == 0:
                            wait_steps(pe, turn, ("dve", "mods", 1))
                        pe.wait_ge(ada_full[k % 2], 16 * (4 * turn + k // 2 + 1))
                        ada_half(banks[7], raw_ada[:, k % 2, :], k).then_inc(ada_used, 1)

            def out(pe, phase, turn, last=False):
                for k in range(4):
                    for part in range(FILL):
                        multiply(pe, phase, turn, k, part, y_hi, y_lo)

            def ba(pe, phase, turn):
                for k in range(2):
                    for part in range(FILL):
                        multiply(pe, phase, turn, k, part, h_hi, h_lo)
                wait_steps(pe, turn, ("dve", "g"))
                for c in range(CHUNKS):
                    mm = nc.tensor.transpose(banks[2][:, c * P:(c + 1) * P], bgT[:, c * P:(c + 1) * P], K["ident"])
                done("pe", "bg", mm)
                wait_steps(pe, turn, ("dve", "bg"))
                for n, masks in enumerate((("le", "ge"), ("gt", "lt"), ("ones", "ones"))):
                    for c in range(CHUNKS):
                        for d in range(2):
                            at = (c * 2 + d) * DN_V_HEADS
                            mm = nc.tensor.matmul(banks[3 + n][:, at:at + DN_V_HEADS], K[masks[d]],
                                                  bg[:, c, 64 + 32 * d:96 + 32 * d], start=True, stop=True)
                    done("pe", f"sums{n}", mm)

            def dn(pe, phase, turn):
                for item in DN_PLANS[phase]:
                    what, arg = item[0], item[1] if len(item) > 1 else None
                    if what == "part":
                        multiply(pe, phase, turn, arg, item[2], h_hi, h_lo)
                    elif what == "decay":
                        wait_steps(pe, turn, ("pool", f"g_mask{arg}"), ring_free(f"decay{arg}"))
                        for d, mask in enumerate(("gt", "lt")):
                            mm = nc.tensor.matmul(ring(f"decay{arg}")[:, 2 * d * P:(2 * d + 2) * P], K[mask],
                                                  g_mask[arg][:, 2 * d:2 * d + 2, :].rearrange("p v i -> p (v i)"),
                                                  start=True, stop=True)
                        done("pe", f"decay{arg}", mm)
                    elif what == "broad":
                        wait_steps(pe, turn, ring_free(f"broad{arg}"))
                        mm = nc.tensor.matmul(ring(f"broad{arg}")[:], K["ones"],
                                              g_mask[arg][:].rearrange("p v i -> p (v i)"), start=True, stop=True)
                        done("pe", f"broad{arg}", mm)
                    elif what == "norms":
                        for n in range(2):
                            wait_steps(pe, turn, ("pool", f"square{n}", True), ring_free(f"ss{n}"))
                            mm = nc.tensor.matmul(ring(f"ss{n}")[:, 0:CONV_OUT], K["ones"], qk_sq[:, n, :], start=True, stop=True)
                            done("pe", f"ss{n}", mm)
                    elif what == "gram":
                        c = arg
                        wait_steps(pe, turn, ring_free(f"gram{c}"), ("dve", "unit1"))
                        kT = dn_qk[:, 1, c * P:(c + 1) * P]
                        bank = ring(f"gram{c}")
                        nc.tensor.matmul(bank[:, 0:P], kT, kT, start=True, stop=True)
                        nc.tensor.matmul(bank[:, P:2 * P], kT, dn_qk[:, 0, c * P:(c + 1) * P], start=True, stop=True)
                        mm = nc.tensor.transpose(bank[:, 2 * P:3 * P], kT, K["ident"])
                        done("pe", f"gram{c}", mm)
                    elif what == "values":
                        wait_steps(pe, turn, ring_free(f"values{arg}"), ("act", f"conv{2 + arg}", True))
                        for c in range(CHUNKS):
                            at = c * P + (PAD if c else 0)
                            mm = nc.tensor.transpose(ring(f"values{arg}")[:, c * P:(c + 1) * P],
                                                     conv[:, 2 + arg, at:at + P], K["ident"])
                        done("pe", f"values{arg}", mm)
                    elif what == "invert":
                        invert(pe, turn, arg, item[2])
                    elif what == "recall":
                        if arg == "B":
                            wait_steps(pe, turn, ring_free("recallB"), ("dve", "stateA"))
                        else:
                            pe.wait_ge(s["state_in"], 16 * (turn + {"dn0": 1, "dn1": GROUP + 1, "dnE": 2 * GROUP}[phase]))
                            wait_steps(pe, turn, ring_free("recallA"))
                        for d in range(2):
                            c = SCAN[arg][d]
                            mm = nc.tensor.matmul(ring(f"recall{arg}")[:, 2 * d * P:(2 * d + 2) * P],
                                                  dn_qk[:, 1, c * P:(c + 1) * P],
                                                  S[:, 2 * d:2 * d + 2, :].rearrange("p v e -> p (v e)"),
                                                  start=True, stop=True)
                        done("pe", f"recall{arg}", mm)
                    elif what == "apply":
                        wait_steps(pe, turn, ring_free(f"apply{arg}"), ("dve", f"xf_{CHUNKS - 1}"),
                                   ("act", "values1") if arg == "0" else ("dve", f"recall{arg}"))
                        for u in range(4):
                            c = SCAN[arg][u // 2]
                            rhs = dn_v[:, 0, u % 2, :] if arg == "0" else R[arg][:, u, :]
                            mm = nc.tensor.matmul(ring(f"apply{arg}")[:, u * P:(u + 1) * P], inv["c", c][:, u, :],
                                                  rhs, start=True, stop=True)
                        done("pe", f"apply{arg}", mm)
                    elif what == "state":
                        if arg == "A":
                            outputs(pe, turn, "A")
                        wait_steps(pe, turn, ring_free(f"state{arg}"), ("dve", f"apply{arg}"))
                        for d in range(2):
                            mm = nc.tensor.matmul(ring(f"state{arg}")[:, 2 * d * P:(2 * d + 2) * P],
                                                  k_nat[:, SCAN[arg][d], :],
                                                  vs[arg][:, 2 * d:2 * d + 2, :].rearrange("p v e -> p (v e)"),
                                                  start=True, stop=True)
                        done("pe", f"state{arg}", mm)
                        if arg == "0":
                            outputs(pe, turn, "0")
                    elif what == "out":
                        outputs(pe, turn, "B")
                    elif what == "out_norm":
                        for v in range(2):
                            wait_steps(pe, turn, ring_free(f"on{v}"), ("act", f"o_sq{v}"))
                            mm = nc.tensor.matmul(ring(f"on{v}")[:, 0:T], K["ones"], o_sq[:, v, :], start=True, stop=True)
                            done("pe", f"on{v}", mm)

            def outputs(pe, turn, step):
                wait_steps(pe, turn, ("act", f"v_new{step}"), ("pool", "q_dec2"), ("dve", "xf_2"),
                           ("dve", "o_n1", True))
                for v in range(2):
                    o = banks[6 + v]
                    for d in range(2):
                        c, u = SCAN[step][d], 2 * d + v
                        mm = nc.tensor.matmul(o[:, c * P:(c + 1) * P], vn[step][:, u, :], decay[c][:, u, :],
                                              start=step == "A" and d == 0, stop=False, skip_group_check=True)
                        if step != "0":
                            mm = nc.tensor.matmul(o[:, c * P:(c + 1) * P], S[:, u, :], q_dec[c][:, u, :],
                                                  start=False, stop=step == "B" and d == 1, skip_group_check=True)
                done("pe", f"out{step}", mm)

            def invert(pe, turn, stage, c):
                g = {n: inv[n, c] for n in ("c", "mt", "mtr", "d", "e", "f", "g", "x")}
                def out_of(name):
                    wait_steps(pe, turn, ring_free(f"{name}_{c}"), *[(e, f"{n}{c}") for e, n in INVERT_NEEDS[name]])
                    return ring(f"{name}_{c}")

                def four(name, lhs, rhs, wide=False):
                    bank = out_of(name)
                    for u in range(4):
                        b = g[rhs][:, u, :]
                        mm = nc.tensor.matmul(bank[:, u * P:(u + 1) * P], g[lhs][:, u, :], b.bitcast(F32) if wide else b,
                                              start=True, stop=True)
                    done("pe", f"{name}_{c}", mm)

                def turned(name, src):
                    bank = out_of(name)
                    for u in range(4):
                        a = g[src][:, u, :]
                        mm = nc.tensor.transpose(bank[:, u * P:(u + 1) * P], a.bitcast(F32) if src == "x" else a, K["ident"])
                    done("pe", f"{name}_{c}", mm)

                for name in INVERT[stage]:
                    if name in ("ct", "xt0"):
                        turned(name, "c" if name == "ct" else "x")
                    elif name == "res":
                        four(name, "mt", "x", wide=True)
                    else:
                        kind = name if name in INVERT_OPERANDS else name.rstrip("0123456789")
                        four(name, *INVERT_OPERANDS[kind])

            run(pe, "pe", {"start": start, "ada": ada, "na": na, "out0": out, "norm1": sum_squares, "ba": ba,
                           "dnP": dn, "dn0": dn, "outA": out, "dn1": dn, "dnE": dn, "outB": out,
                           "norm2": sum_squares})

        @block.scalar
        def _(act):
            act.sem_inc(s["scalar_steps"], CREDIT)

            def squares_of_x(act, phase, turn):
                for k in range(KT):
                    if k >= 2:
                        wait_steps(act, turn, ("pe", f"squared{k - 2}"))
                    done("act", f"square{k}", nc.scalar.activation(squares[:, k % 2, :], x[:, k, :], ACT.Square))
                wait_steps(act, turn, ("pe", f"squared{KT - 1}"))
                done("act", "log", nc.scalar.activation(logs[:], banks[2][:, 0:T], ACT.Ln, bias=bias_eps[:, 0:1],
                                                        scale=1.0 / D_MODEL))
                wait_steps(act, turn, ("act", "log"))
                done("act", "rstd", nc.scalar.activation(rstd[:], logs[:], ACT.Exp, scale=-0.5))

            def start(act, phase, turn):
                small = [(consts[:], "consts"), (cond[:], "cond"), (ada_b[:], "ada_b"), (norm_w[:], "norm_w"),
                         (cache_k[:], "cache_k"), (cache_v[:], "cache_v"),
                         (conv_w[:], "conv_w"), (alog_dt[:, 0:2], "alog_dt"), (dn_norm_w[:], "dn_norm_w")]
                for dst, name in small:
                    act.dma_start(dst, dram[name]).then_inc(s["small_in"], 16)
                act.dma_start(x[:], dram["x"]).then_inc(s["small_in"], 16)
                for row in range(ROWS):
                    for keys in range(ROWS):
                        rel = bass.AP(dram["rpb"].tensor, (ROWS - 1 - row + keys) * GRID_W * BIAS_W + GRID_W - 1,
                                      [[BIAS_W - 1, GRID_W], [(2 * ROWS - 1) * GRID_W * BIAS_W, NA_HEADS], [1, GRID_W]])
                        dst = bias[(row % 2) * GRID_W:(row % 2 + 1) * GRID_W, row // 2, :,
                                   keys * GRID_W:(keys + 1) * GRID_W]
                        act.dma_start(dst, rel).then_inc(s["small_in"], 16)
                act.wait_ge(s["small_in"], 16 * SMALL_LOADS)
                done("act", "cond", nc.scalar.activation(cond[:], cond[:], ACT.Silu))
                wait_steps(act, turn, ("dve", "consts"))
                squares_of_x(act, phase, turn)

            def modulate(act, phase, turn):
                for k in range(KT):
                    wait_steps(act, turn, ("dve", f"scaled{k}"))
                    if k >= 2:
                        wait_steps(act, turn, ("dve", f"lo{k - 2}"))
                    layer = 0 if phase == "mod0" else 1
                    for g, sl in ((0, slice(0, CTX)), (1, slice(CTX, T))):
                        i = nc.scalar.activation(shifted[:, k % 2, sl], scaled[:, k % 2, sl], ACT.Identity,
                                                 bias=mods[:, layer * 3 * KT + k, g:g + 1], scale=gain[:, k, g:g + 1])
                    done("act", f"shifted{k}", i)
                if phase == "mod0":
                    for k in range(LOOKAHEAD):
                        split_hi(act, "na", 0, k)

            def na(act, phase, turn):
                for item in NA_PLAN:
                    if item[0] == "part" and item[2] == 0:
                        k = item[1]
                        split_hi(act, phase, turn, k + LOOKAHEAD)
                        if k == 2:
                            bank = tile_done(act, phase, turn, 0)
                            nc.scalar.activation(qk[:, 0, :], bank[:, 0:T], ACT.Copy, scale=SCALE).then_inc(s["evacuated"], 1)
                        elif k == 4:
                            bank = tile_done(act, phase, turn, 1)
                            wait_steps(act, turn, ("pool", "cache_k1"))
                            nc.scalar.activation(qk[:, 1, :], bank[:, 0:T], ACT.Copy).then_inc(s["evacuated"], 1)
                        elif k == 6:
                            bank = tile_done(act, phase, turn, 2)
                            wait_steps(act, turn, ("pool", "cache_v1"))
                            nc.scalar.activation(vT[:], bank[:, 0:T], ACT.Copy).then_inc(s["evacuated"], 1)
                    elif item[0] == "scores":
                        for r in range(3):
                            wait_steps(act, turn, ("dve", f"max{r}"))
                            wide = slice(0, CTX) if r == 0 else slice(0, T)
                            dst = probs[:, 0:CTX] if r == 0 else probs[:, CTX + (r - 1) * T:CTX + r * T]
                            if r == 0:
                                wait_steps(act, turn, ("pe", "probsT1", 1))
                            done("act", f"exp{r}", nc.scalar.activation(
                                dst, banks[2 + r][:, wide], ACT.Exp, bias=stats[:, 0, r:r + 1],
                                accum_out=stats[:, 1, r:r + 1]))
                    elif item[0] == "values":
                        wait_steps(act, turn, ("pe", "values"))
                        done("act", "V", nc.scalar.activation(V[:].rearrange("p c d -> p (c d)"), banks[5][:, 0:T], ACT.Copy))
                    elif item[0] == "turn_probs":
                        bank = tile_done(act, phase, turn, 3)
                        wait_steps(act, turn, ("dve", "y", 1))
                        nc.scalar.activation(gate_na[:], bank[:, 0:T], ACT.Silu).then_inc(s["evacuated"], 1)

            def y_high(act, phase, turn):
                at = 2 if phase == "ysplitA" else 0
                for k in range(0, KT, 4):
                    done("act", f"y_hi{k}", nc.scalar.activation(y_hi[:, k:k + 4, :], y[:, at + k:at + k + 4, :], ACT.Copy))

            def out(act, phase, turn, last=False):
                for k in range(4):
                    if not last or k + LOOKAHEAD < 4:
                        split_hi(act, phase, turn, k + LOOKAHEAD)

            def ba(act, phase, turn):
                for k in range(2):
                    split_hi(act, phase, turn, k + LOOKAHEAD)
                bank = tile_done(act, phase, turn, 0)
                done("act", "exp_b", nc.scalar.activation(bt[0:64, :], bank[0:64, 0:T], ACT.Exp, scale=-1.0))
                act.wait_ge(s["small_in"], 16 * SMALL_LOADS)
                nc.scalar.activation(bt2[64:128, :], bank[64:128, 0:T], ACT.Identity,
                                     bias=alog_dt[64:128, 1:2]).then_inc(s["evacuated"], 1)
                tile_read(act, phase, turn, 0)
                done("act", "abs", nc.scalar.activation(bgT[64:128, :], bt2[64:128, :], ACT.Abs))
                wait_steps(act, turn, ("act", "abs"))
                done("act", "exp_g", nc.scalar.activation(bt[64:128, :], bgT[64:128, :], ACT.Exp, scale=-1.0))
                wait_steps(act, turn, ("act", "exp_g"))
                done("act", "log1p", nc.scalar.activation(bgT[64:128, :], bt[64:128, :], ACT.Ln, bias=1.0))
                done("act", "rate", nc.scalar.activation(alog_dt[64:128, 2:3], alog_dt[64:128, 0:1], ACT.Exp))
                for n, dst in enumerate((neg_egc, beta_egl, egl)):
                    wait_steps(act, turn, ("pe", f"sums{n}"))
                    done("act", f"table{n}", nc.scalar.activation(dst[:].rearrange("p c d h -> p (c d h)"),
                                                                  banks[3 + n][:, 0:CHUNKS * 2 * DN_V_HEADS], ACT.Exp))

            def dn(act, phase, turn):
                head, _, _, row = heads(phase, turn)
                if head is not None:
                    wait_steps(act, turn, ("pe", "outB", 1), ("dve", "stateA", 1))
                    act.dma_start(S[:], dram["state"][bass.ds(head, 1)].rearrange("a p u e -> p (a u) e"))\
                        .then_inc(s["state_in"], 16)

                def copy(name, dst, src, *others):
                    wait_steps(act, turn, ("pe", name), *others)
                    done("act", name, nc.scalar.activation(dst, src, ACT.Copy))

                for item in DN_PLANS[phase]:
                    what, arg = item[0], item[1] if len(item) > 1 else None
                    if what == "part" and item[2] == 0:
                        split_hi(act, phase, turn, arg + LOOKAHEAD)
                        if arg in (2, 4, 6, 8):
                            j = arg // 2 - 1
                            bank = tile_done(act, phase, turn, j)
                            wait_steps(act, turn, ("dve", f"conv{(j + 2) % 4}", j < 2))
                            nc.scalar.activation(padded[:, j % 2, PAD:PAD + CTX], bank[:, 0:CTX], ACT.Copy)
                            nc.scalar.activation(padded[:, j % 2, LAT_AT:LAT_AT + LAT], bank[:, CTX:T], ACT.Copy)\
                                .then_inc(s["evacuated"], 1)
                    if what == "part" and item[2] == 2 and arg in (5, 7, 9, 11):
                        j = arg // 2 - 2
                        wait_steps(act, turn, ("dve", f"conv{j}"))
                        i = nc.scalar.activation(conv[:, j, :], conv[:, j, :], ACT.Silu)
                        done("act", f"conv{j}", i)
                    if what == "part" and item[2] == FILL // 2 and arg == 10:
                        bank = tile_done(act, phase, turn, 4)
                        nc.scalar.activation(y_row(row), bank[:, 0:T], ACT.Silu).then_inc(s["evacuated"], 1)
                    if what == "decay":
                        wait_steps(act, turn, ("pe", f"decay{arg}"), ("pe", "outB", 1))
                        done("act", f"decay{arg}", nc.scalar.activation(decay[arg][:].rearrange("p u i -> p (u i)"),
                                                                        ring(f"decay{arg}")[:], ACT.Exp))
                    elif what == "broad":
                        wait_steps(act, turn, ("pe", f"broad{arg}"))
                        done("act", f"broad{arg}", nc.scalar.activation(q_dec[arg][:].rearrange("p u i -> p (u i)"),
                                                                        ring(f"broad{arg}")[:], ACT.Exp))
                    elif what == "norms":
                        for n in range(2):
                            wait_steps(act, turn, ("pe", f"ss{n}"))
                            done("act", f"ss{n}", nc.scalar.activation(qk_rs[:, n, :], ring(f"ss{n}")[:, 0:CONV_OUT],
                                                                       ACT.Ln, bias=bias_eps[:, 0:1]))
                        for n in range(2):
                            wait_steps(act, turn, ("act", f"ss{n}"))
                            extra = {"bias": bias_eps[:, 1:2]} if n == 0 else {}
                            done("act", f"rs{n}", nc.scalar.activation(qk_rs[:, n, :], qk_rs[:, n, :], ACT.Exp,
                                                                       scale=-0.5, **extra))
                    elif what == "gram":
                        c = arg
                        wait_steps(act, turn, ("pe", f"gram{c}"), ("dve", f"gram{c}"), ("pe", "stateA", True),
                                   ("pe", "state0", True))
                        done("act", f"gram{c}", nc.scalar.activation(k_nat[:, c, :], ring(f"gram{c}")[:, 2 * P:3 * P],
                                                                     ACT.Copy))
                    elif what == "values":
                        copy(f"values{arg}", dn_v[:, :, arg, :],
                             ring(f"values{arg}")[:, 0:T].rearrange("p (c e) -> p c e", c=CHUNKS),
                             ("dve", "recallB", True), ("pe", "apply0", True))
                    elif what == "invert":
                        c = item[2]
                        for name in INVERT[arg]:
                            if name in READ_BY_SCALAR:
                                slot = {"p2": "f", "p2t": "g", "p4": "d", "p4t": "e", "p8t": "f"}.get(
                                    name, "g" if name.startswith("xt") else "x")
                                others = []
                                if name == "xt0":
                                    others = [("dve", f"x1_{c}")]
                                elif name == "p4":
                                    others = [("pool", f"x0{c}")]
                                elif name.startswith("xn"):
                                    others = [("pe", f"xt{name[2:]}_{c}")]
                                copy(f"{name}_{c}", inv[slot, c][:].rearrange("p u i -> p (u i)"),
                                     ring(f"{name}_{c}")[:], *others)
                        if arg == 1:
                            wait_steps(act, turn, ("dve", f"ct_{c}"), ("pool", f"near{c}"))
                            done("act", f"mtr{c}", nc.scalar.activation(inv["mtr", c][:], inv["mt", c][:], ACT.Copy))
                    elif what == "apply":
                        wait_steps(act, turn, ("pe", f"apply{arg}"))
                        for u in range(4):
                            c, d = SCAN[arg][u // 2], u // 2
                            i = nc.scalar.activation(vn[arg][:, u, :], ring(f"apply{arg}")[:, u * P:(u + 1) * P],
                                                     ACT.Copy, scale=beta_now[:, c, d, u % 2:u % 2 + 1])
                        done("act", f"v_new{arg}", i)
                    elif what == "state" and arg == "0":
                        copy("state0", s_out[:].rearrange("p u e -> p (u e)"), ring("state0")[:])
                        wait_steps(act, turn, ("act", "state0"))
                        act.dma_start(dram["state_out"][bass.ds(head, 1)].rearrange("a p u e -> p (a u) e"), s_out[:])\
                            .then_inc(s["state_out"], 16)
                    elif what == "out_norm":
                        wait_steps(act, turn, ("pe", "outB"))
                        for v in range(2):
                            done("act", f"o_sq{v}", nc.scalar.activation(o_sq[:, v, :], banks[6 + v][:, 0:T], ACT.Square))
                        for v in range(2):
                            wait_steps(act, turn, ("pe", f"on{v}"))
                            done("act", f"on{v}", nc.scalar.activation(o_rs[:, v, :], ring(f"on{v}")[:, 0:T], ACT.Ln,
                                                                       bias=bias_eps[:, 0:1], scale=1.0 / P))
                        for v in range(2):
                            wait_steps(act, turn, ("act", f"on{v}"))
                            done("act", f"o_rs{v}", nc.scalar.activation(o_rs[:, v, :], o_rs[:, v, :], ACT.Exp, scale=-0.5))
                        act.wait_ge(s["state_out"], 16 * (head + 1))
                    elif what == "gates":
                        bank = tile_done(act, phase, turn, 5)
                        nc.scalar.activation(y_row(row + 1), bank[:, 0:T], ACT.Silu).then_inc(s["evacuated"], 1)

            def kept(act, phase, turn):
                act.wait_ge(s["x_out"], 16 if phase == "keep0" else 32)

            def final(act, phase, turn):
                for k in range(KT):
                    wait_steps(act, turn, ("dve", f"final{k}"))
                    act.dma_start(dram["y_out"][:, k, :], x[:, k, :]).then_inc(s["y_out"], 16)
                act.wait_ge(s["y_out"], 16 * KT)
                act.wait_ge(s["k_out"], 16 * NA_HEADS)
                act.wait_ge(s["v_out"], 16 * NA_HEADS)
                act.wait_ge(s["state_out"], 16 * DN_K_HEADS)

            run(act, "act", {"start": start, "mod0": modulate, "na": na, "ysplit0": y_high, "out0": out,
                             "norm1": squares_of_x, "mod1": modulate, "ba": ba, "keep0": kept, "dnP": dn,
                             "dn0": dn, "ysplitA": y_high, "outA": out, "keep1": kept, "dn1": dn, "dnE": dn,
                             "ysplitB": y_high, "outB": out, "norm2": squares_of_x, "final": final})

        @block.vector
        def _(dve):
            dve.sem_inc(s["vector_steps"], CREDIT)
            for n in range(RAW_SLOTS):
                dve.sem_inc(consumed[n], 1)

            def start(dve, phase, turn):
                nc.vector.memset(bias_eps[:, 0:1], EPS)
                done("dve", "consts", nc.vector.memset(bias_eps[:, 1:2], float(np.log(SCALE))))
                dve.wait_ge(s["small_in"], 16 * SMALL_LOADS)
                done("dve", "twice", nc.vector.tensor_scalar(twice[:], K["ident"], 2.0, None, ALU.mult))

            def ada(dve, phase, turn):
                for g in range(2):
                    half_used(dve, phase, turn, 8 * g + 7)
                    at = 8 * turn + 4 * g
                    done("dve", f"mods{g}", nc.vector.tensor_tensor(
                        mods[:, bass.ds(at, 4), :], banks[4 + g][:, 0:8].rearrange("p (a b) -> p a b", b=2),
                        ada_b[:, bass.ds(at, 4)].unsqueeze(2).broadcast_to([P, 4, 2]), ALU.add))

            def modulate(dve, phase, turn):
                layer = 0 if phase == "mod0" else 1
                at = layer * 3 * KT + KT
                done("dve", "one", nc.vector.tensor_scalar(gain[:], mods[:, at:at + KT, :], 1.0, None, ALU.add))
                wait_steps(dve, turn, ("dve", "one"))
                done("dve", "gain", nc.vector.tensor_tensor(
                    gain[:], gain[:], norm_w[:, layer, :].unsqueeze(2).broadcast_to([P, KT, 2]), ALU.mult))
                wait_steps(dve, turn, ("dve", "gain"))

                def low(k):
                    wait_steps(dve, turn, ("pool", f"hi{k}"))
                    done("dve", f"lo{k}", nc.vector.tensor_tensor(h_lo[:, k, :], shifted[:, k % 2, :],
                                                                  h_hi[:, k, :].bitcast(F32), ALU.subtract))
                for k in range(KT):
                    if k >= 2:
                        wait_steps(dve, turn, ("act", f"shifted{k - 2}"))
                    done("dve", f"scaled{k}", nc.vector.tensor_tensor(scaled[:, k % 2, :], x[:, k, :], rstd[:], ALU.mult))
                    if k >= 1:
                        low(k - 1)
                low(KT - 1)
                if phase == "mod0":
                    for k in range(LOOKAHEAD):
                        split_lo(dve, "na", 0, k)

            def na(dve, phase, turn):
                for item in NA_PLAN:
                    if item[0] == "part" and item[2] == 0:
                        split_lo(dve, phase, turn, item[1] + LOOKAHEAD)
                    elif item[0] == "scores":
                        for r in range(3):
                            wait_steps(dve, turn, ("pe", f"scores{r}"))
                            if r:
                                local = banks[2 + r][:, 0:LAT]
                                done("dve", f"biased{r}", nc.vector.tensor_tensor(
                                    local, local, bias[:, r - 1, bass.ds(turn, 1), :].rearrange("p a k -> p (a k)"), ALU.add))
                                wait_steps(dve, turn, ("dve", f"biased{r}"))
                            else:
                                wait_steps(dve, turn, ("pool", "probs2", 1))
                            wide = slice(0, CTX) if r == 0 else slice(0, T)
                            done("dve", f"max{r}", nc.vector.tensor_reduce(stats[:, 0, r:r + 1], banks[2 + r][:, wide],
                                                                           AX_X, ALU.max, negate=True))
                        for r in range(3):
                            wait_steps(dve, turn, ("act", f"exp{r}"))
                            done("dve", f"rsum{r}", nc.vector.reciprocal(stats[:, 2, r:r + 1], stats[:, 1, r:r + 1]))
                    elif item[0] == "turn_probs":
                        for n in range(2):
                            wait_steps(dve, turn, ("pe", f"probsT{n}"), ("pe", "attend", True))
                            dst = probsT[:, 0:CTX + LAT] if n == 0 else probsT[:, CTX + LAT:CTX + 3 * LAT]
                            src = banks[6][:, 0:CTX + LAT] if n == 0 else banks[2][:]
                            done("dve", f"probsT{n}", nc.vector.tensor_copy(dst, src))
                    elif item[0] == "attend":
                        wait_steps(dve, turn, ("pe", "attend"))
                        tile_read(dve, phase, turn, 3)
                        done("dve", "y", nc.vector.tensor_tensor(
                            y_row(turn), banks[3][:, 0:T], gate_na[:], ALU.mult))
                dve.wait_ge(ada_used, 8 * turn + 8 + 2)
                at = 4 * turn + 2 * KT
                done("dve", "mods", nc.vector.tensor_tensor(
                    mods[:, bass.ds(at, 4), :], banks[7][:, 0:8].rearrange("p (a b) -> p a b", b=2),
                    ada_b[:, bass.ds(at, 4)].unsqueeze(2).broadcast_to([P, 4, 2]), ALU.add))

            def y_low(dve, phase, turn):
                at = 2 if phase == "ysplitA" else 0
                for k in range(0, KT, 4):
                    wait_steps(dve, turn, ("act", f"y_hi{k}"))
                    done("dve", f"y_lo{k}", nc.vector.tensor_tensor(y_lo[:, k:k + 4, :], y[:, at + k:at + k + 4, :],
                                                                    y_hi[:, k:k + 4, :].bitcast(F32), ALU.subtract))

            def out(dve, phase, turn, last=False):
                layer = 0 if phase == "out0" else 1
                dve.wait_ge(s["x_in"], {"out0": 16, "outA": 32, "outB": 48}[phase])
                for k in range(4):
                    if not last or k + LOOKAHEAD < 4:
                        split_lo(dve, phase, turn, k + LOOKAHEAD)
                    if k % 2:
                        tile = k // 2
                        bank = tile_done(dve, phase, turn, tile)
                        m = 2 * turn + tile
                        for g, sl in ((0, slice(0, CTX)), (1, slice(CTX, T))):
                            xs = x[:, bass.ds(m, 1), sl].rearrange("p a t -> p (a t)")
                            gate = mods[:, bass.ds(m + (layer * 3 + 2) * KT, 1), g:g + 1].rearrange("p a b -> p (a b)")
                            i = nc.vector.scalar_tensor_tensor(xs, bank[:, sl], gate, xs, ALU.mult, ALU.add)
                        i.then_inc(s["evacuated"], 1)

            def ba(dve, phase, turn):
                for k in range(2):
                    split_lo(dve, phase, turn, k + LOOKAHEAD)
                wait_steps(dve, turn, ("act", "exp_b"))
                done("dve", "plus", nc.vector.tensor_scalar(bt[0:64, :], bt[0:64, :], 1.0, None, ALU.add))
                wait_steps(dve, turn, ("dve", "plus"))
                done("dve", "beta", nc.vector.reciprocal(bgT[0:64, :], bt[0:64, :]))
                wait_steps(dve, turn, ("act", "rate"))
                done("dve", "softplus", nc.vector.scalar_tensor_tensor(bt[64:128, :], bt2[64:128, :], 0.0, bgT[64:128, :],
                                                                       ALU.max, ALU.add))
                wait_steps(dve, turn, ("dve", "softplus"))
                done("dve", "g", nc.vector.tensor_scalar(bgT[64:128, :], bt[64:128, :], alog_dt[64:128, 2:3], -1.0,
                                                         ALU.mult, ALU.mult))
                wait_steps(dve, turn, ("pe", "bg"))
                done("dve", "bg", nc.vector.tensor_copy(bg[:].rearrange("p c h -> p (c h)"), banks[2][:, 0:T]))
                wait_steps(dve, turn, ("act", "table1"), ("dve", "bg"))
                done("dve", "neg_egc", nc.vector.tensor_scalar(neg_egc[:], neg_egc[:], -1.0, None, ALU.mult))
                done("dve", "beta_egl", nc.vector.tensor_tensor(
                    beta_egl[:].rearrange("p c d h -> p c (d h)"), beta_egl[:].rearrange("p c d h -> p c (d h)"),
                    bg[:, :, 0:64], ALU.mult))

            def pads(dve, phase, turn):
                nc.vector.memset(padded[:, :, 0:PAD], 0.0)
                nc.vector.memset(padded[:, :, PAD + CTX:LAT_AT], 0.0)
                done("dve", "pads", nc.vector.memset(padded[:, :, LAT_AT + LAT:PADDED], 0.0))

            def dn(dve, phase, turn):
                head, next_head, _, _ = heads(phase, turn)

                def table(t, c, d, v):
                    return t[:, c, d, bass.ds(2 * head + v, 1)]

                if head is not None:
                    wait_steps(dve, turn, ("act", "v_newB", 1))
                    done("dve", "beta_now", nc.vector.tensor_copy(
                        beta_now[:], bg[:, :, 0:64].rearrange("p c (d h) -> p c d h", d=2)[:, :, :, bass.ds(2 * head, 2)]))

                    wait_steps(dve, turn, ("pool", "g_mask2", 1))
                    done("dve", "g_now", nc.vector.tensor_copy(
                        g_now[:], bg[:, :, 64:P].rearrange("p c (d h) -> p c d h", d=2)[:, :, :, bass.ds(2 * head, 2)]))

                for item in DN_PLANS[phase]:
                    what, arg = item[0], item[1] if len(item) > 1 else None
                    if what == "part" and item[2] == 0:
                        split_lo(dve, phase, turn, arg + LOOKAHEAD)
                    at = FILL * arg + item[2] - TAPS_AT if what == "part" else -1
                    if at >= 0 and at % (2 * FILL) < CONV and at < 4 * 2 * FILL:
                        j, t = divmod(at, 2 * FILL)
                        if t == 0:
                            tile_read(dve, phase, turn, j)
                            if j < 2:
                                wait_steps(dve, turn, ("pool", f"square{j}", True), ("dve", f"unit{j}"))
                            else:
                                wait_steps(dve, turn, ("pe", f"values{j - 2}"))
                        else:
                            wait_steps(dve, turn, ("dve", f"tap{j}{t - 1}"))
                        w = conv_w[:, bass.ds(next_head, 1), j, t:t + 1].rearrange("p a b -> p (a b)")
                        src = padded[:, j % 2, t:t + CONV_OUT]
                        dst = conv[:, j, :]
                        if t == 0:
                            i = nc.vector.tensor_scalar(dst, src, w, None, ALU.mult)
                        else:
                            i = nc.vector.scalar_tensor_tensor(dst, src, w, dst, ALU.mult, ALU.add)
                        done("dve", f"tap{j}{t}" if t < CONV - 1 else f"conv{j}", i)
                    if what == "unit":
                        for n in range(2):
                            wait_steps(dve, turn, ("act", f"rs{n}"), ("pe", "recallB", True), ("pool", "q_dec2", True))
                            nc.vector.tensor_tensor(dn_qk[:, n, 0:CTX], conv[:, n, 0:CTX], qk_rs[:, n, 0:CTX], ALU.mult)
                            done("dve", f"unit{n}", nc.vector.tensor_tensor(
                                dn_qk[:, n, CTX:T], conv[:, n, CTX + PAD:CONV_OUT], qk_rs[:, n, CTX + PAD:CONV_OUT], ALU.mult))
                    elif what == "gram":
                        c = arg
                        wait_steps(dve, turn, ("pe", f"gram{c}"))
                        both = ring(f"gram{c}")[:, 0:2 * P].rearrange("p (n i) -> p n i", n=2)
                        done("dve", f"gram{c}", nc.vector.tensor_tensor(
                            gram[:], both.unsqueeze(2).broadcast_to([P, 2, 2, P]),
                            consts[:, CONSTS.index("lt"):CONSTS.index("lt") + 4, :]
                            .rearrange("p (n d) i -> p n d i", n=2), ALU.mult))
                        wait_steps(dve, turn, ("dve", f"gram{c}"), ("act", f"decay{c}"), ("pe", f"broad{max(c, 1)}"),
                                   ("pe", "applyB", True))
                        for u in range(4):
                            i = nc.vector.scalar_tensor_tensor(inv["c", c][:, u, :], decay[c][:, u, :],
                                                               beta_now[:, c, u // 2, u % 2:u % 2 + 1],
                                                               gram[:, 0, u // 2, :], ALU.mult, ALU.mult)
                        done("dve", f"c{c}", i)
                        wait_steps(dve, turn, ("dve", f"c{c}"))
                        both = decay[c][:].rearrange("p (d v) i -> p d v i", d=2)
                        done("dve", f"masked{c}", nc.vector.tensor_tensor(
                            both, both, gram[:, 1, :, :].unsqueeze(2).broadcast_to([P, 2, 2, P]), ALU.mult))
                        wait_steps(dve, turn, ("dve", f"masked{c}"))
                    elif what == "invert":
                        invert(dve, turn, arg, item[2])
                    elif what == "recall":
                        wait_steps(dve, turn, ("pe", f"recall{arg}"))
                        for u in range(4):
                            c = SCAN[arg][u // 2]
                            i = nc.vector.scalar_tensor_tensor(R[arg][:, u, :], ring(f"recall{arg}")[:, u * P:(u + 1) * P],
                                                               table(neg_egc, c, u // 2, u % 2), dn_v[:, c, u % 2, :],
                                                               ALU.mult, ALU.add)
                        done("dve", f"recall{arg}", i)
                    elif what == "apply" and arg != "B":
                        wait_steps(dve, turn, ("act", f"v_new{arg}"))
                        for u in range(4):
                            i = nc.vector.tensor_scalar(vs[arg][:, u, :], ring(f"apply{arg}")[:, u * P:(u + 1) * P],
                                                        table(beta_egl, SCAN[arg][u // 2], u // 2, u % 2), None, ALU.mult)
                        done("dve", f"apply{arg}", i)
                    elif what == "state" and arg == "A":
                        wait_steps(dve, turn, ("pe", "stateA"), ("pe", "outA"))
                        for u in range(4):
                            i = nc.vector.scalar_tensor_tensor(S[:, u, :], S[:, u, :],
                                                               table(egl, SCAN["A"][u // 2], u // 2, u % 2),
                                                               ring("stateA")[:, u * P:(u + 1) * P], ALU.mult, ALU.add)
                        done("dve", "stateA", i)
                    elif what == "out_norm":
                        for v in range(2):
                            wait_steps(dve, turn, ("act", f"o_rs{v}"))
                            done("dve", f"o_n{v}", nc.vector.scalar_tensor_tensor(
                                o_n[:, v, :], banks[6 + v][:, 0:T], dn_norm_w[:, 0:1], o_rs[:, v, :], ALU.mult, ALU.mult))

            def invert(dve, turn, stage, c):
                wide = [P, 4, P]
                ident = K["ident"].unsqueeze(1).broadcast_to(wide)
                near = K["near"].unsqueeze(1).broadcast_to(wide)
                two = twice[:].unsqueeze(1).broadcast_to(wide)

                def psum(name):
                    wait_steps(dve, turn, ("pe", f"{name}_{c}"))
                    return ring(f"{name}_{c}")[:].rearrange("p (u i) -> p u i", u=4)

                if stage == 0:
                    src = psum("ct")
                    done("dve", f"near{c}", nc.vector.tensor_tensor(inv["e", c][:], src, near, ALU.mult))
                    done("dve", f"ct_{c}", nc.vector.tensor_tensor(inv["mt", c][:], src, ident, ALU.add))
                for name in INVERT[stage]:
                    if name in ("x1", "x2", "x3"):
                        src = psum(name)
                        done("dve", f"{name}_{c}", nc.vector.tensor_tensor(inv["x", c][:], src, inv["x", c][:].bitcast(F32),
                                                                          ALU.add))
                        wait_steps(dve, turn, ("dve", f"{name}_{c}"))
                    elif name[0] == "t" or name == "res":
                        src = psum(name)
                        done("dve", f"{name}_{c}", nc.vector.scalar_tensor_tensor(
                            inv["d", c][:], src, -1.0, ident if name == "res" else two, ALU.mult, ALU.add))
                    elif name == "xf":
                        src = psum(name)
                        done("dve", f"xf_{c}", nc.vector.tensor_tensor(inv["c", c][:], src, inv["x", c][:].bitcast(F32), ALU.add))

            def final(dve, phase, turn):
                for k in range(KT):
                    done("dve", f"final{k}", nc.vector.scalar_tensor_tensor(x[:, k, :], x[:, k, :], norm_w[:, 2, k:k + 1],
                                                                            rstd[:], ALU.mult, ALU.mult))

            run(dve, "dve", {"start": start, "ada": ada, "mod0": modulate, "na": na, "ysplit0": y_low, "out0": out,
                             "mod1": modulate, "ba": ba, "keep0": pads, "dnP": dn, "dn0": dn,
                             "ysplitA": y_low, "outA": out, "keep1": pads, "dn1": dn, "dnE": dn, "ysplitB": y_low, "outB": out, "final": final})

        @block.gpsimd
        def _(pool):
            pool.sem_inc(s["pool_steps"], CREDIT)

            def lone():
                pool.sem_inc(s["pool_waits"], 1)

            def start(pool, phase, turn):
                pool.wait_ge(s["small_in"], 16 * SMALL_LOADS)
                for r in range(2):
                    grid = K["grid"][:, 0:GRID_W].unsqueeze(1).broadcast_to([P, NA_HEADS * ROWS, GRID_W])
                    b = bias[:, r, :, :].rearrange("p h (i k) -> p (h i) k", i=ROWS)
                    done("pool", f"masked{r}", nc.gpsimd.tensor_tensor(b, b, grid, ALU.add))

            def modulate(pool, phase, turn):
                for k in range(KT):
                    wait_steps(pool, turn, ("act", f"shifted{k}"))
                    done("pool", f"hi{k}", nc.gpsimd.tensor_copy(h_hi[:, k, :], shifted[:, k % 2, :]))

            def na(pool, phase, turn):
                def load_ada(k):
                    pool.wait_ge(ada_used, 8 * turn + k + 1)
                    lone()
                    pool.dma_start(raw_ada[:, k % 2, :],
                                   dram["late"][bass.ds(8 * turn + k, 1)].rearrange("a p f -> p (a f)"))\
                        .then_inc(ada_full[k % 2], 16)

                load_ada(0)
                load_ada(1)
                wait_steps(pool, turn, ("pe", "scores2", 1))
                lone()
                done("pool", "cache_k1", nc.gpsimd.tensor_copy(
                    cache_k1[:], cache_k[:, bass.ds(turn, 1), :].rearrange("p a k -> p (a k)")))
                wait_steps(pool, turn, ("pe", "attend", 1))
                lone()
                done("pool", "cache_v1", nc.gpsimd.tensor_copy(
                    cache_v1[:], cache_v[:, bass.ds(turn, 1), :].rearrange("p a k -> p (a k)")))
                for item in NA_PLAN:
                    if item[0] == "ada" and item[1] < 6:
                        load_ada(item[1] + 2)
                    elif item[0] == "scores":
                        tile_read(pool, phase, turn, 1)
                        lone()
                        pool.dma_start(dram["k_out"][bass.ds(turn, 1)].rearrange("a p t -> p (a t)"), qk[:, 1, 0:CTX])\
                            .then_inc(s["k_out"], 16)
                        for r in range(3):
                            wait_steps(pool, turn, ("dve", f"rsum{r}"))
                            lone()
                            p = probs[:, 0:CTX] if r == 0 else probs[:, CTX + (r - 1) * T:CTX + r * T]
                            done("pool", f"probs{r}", nc.gpsimd.tensor_scalar(p, p, stats[:, 2, r:r + 1], 1.0,
                                                                              ALU.mult, ALU.mult))
                    elif item[0] == "values":
                        tile_read(pool, phase, turn, 2)
                        lone()
                        pool.dma_start(dram["v_out"][bass.ds(turn, 1)].rearrange("a p t -> p (a t)"), vT[:, 0:CTX])\
                            .then_inc(s["v_out"], 16)
                pool.wait_ge(s["k_out"], 16 * (turn + 1))
                pool.wait_ge(s["v_out"], 16 * (turn + 1))

            def fetch(pool, phase, turn):
                pool.dma_start(x[:], dram["x"] if phase == "fetch0" else dram["x_kept"]).then_inc(s["x_in"], 16)

            def keep(pool, phase, turn):
                pool.dma_start(dram["x_kept"], x[:]).then_inc(s["x_out"], 16)
                if phase == "keep1":
                    square_qk(pool, turn)
                pool.wait_ge(s["x_out"], 16 if phase == "keep0" else 32)

            def square_qk(pool, turn, *which):
                for n in range(2):
                    wait_steps(pool, turn, ("act", f"conv{n}"), *which)
                    done("pool", f"square{n}", nc.gpsimd.tensor_tensor(qk_sq[:, n, :], conv[:, n, :], conv[:, n, :],
                                                                      ALU.mult))

            def dn(pool, phase, turn):
                head, _, row, _ = heads(phase, turn)
                for item in DN_PLANS[phase]:
                    what, arg = item[0], item[1] if len(item) > 1 else None
                    if what == "squares" and phase != "dnE":
                        square_qk(pool, turn, ("pe", "applyB"))
                    elif what == "decay":
                        wait_steps(pool, turn, ("pe", "applyB", True), ("dve", "g_now"))
                        lone()
                        for u in range(4):
                            d, v = u // 2, u % 2
                            i = nc.gpsimd.tensor_scalar(g_mask[arg][:, u, :], K["le" if d == 0 else "ge"],
                                                        g_now[:, arg, d, v:v + 1], 1.0, ALU.mult, ALU.mult)
                        done("pool", f"g_mask{arg}", i)
                    elif what == "gram":
                        near = K["near"].unsqueeze(1).broadcast_to([P, 4, P])
                        ident = K["ident"].unsqueeze(1).broadcast_to([P, 4, P])
                        wait_steps(pool, turn, ("dve", f"c{arg}"))
                        done("pool", f"near{arg}", nc.gpsimd.tensor_tensor(inv["d", arg][:], inv["c", arg][:], near, ALU.mult))
                        if arg < CHUNKS - 1:
                            continue
                        for c in range(CHUNKS):
                            wait_steps(pool, turn, ("pool", f"near{c}"))
                            done("pool", f"x0{c}", nc.gpsimd.tensor_tensor(inv["x", c][:], ident,
                                                                          inv["d", c][:].bitcast(F32), ALU.subtract))
                        for c in (1, 2):
                            wait_steps(pool, turn, ("act", f"broad{c}"))
                            q = dn_qk[:, 0, c * P:(c + 1) * P].unsqueeze(1).broadcast_to([P, 4, P])
                            done("pool", f"q_dec{c}", nc.gpsimd.tensor_tensor(q_dec[c][:], q_dec[c][:], q, ALU.mult))
                    elif what == "out_norm":
                        for v in range(2):
                            wait_steps(pool, turn, ("dve", f"o_n{v}"))
                            if phase != "dnE":
                                tile_read(pool, phase, turn, -1)
                            done("pool", f"y{v}", nc.gpsimd.tensor_tensor(
                                y_row(row + v), y_row(row + v), o_n[:, v, :], ALU.mult))

            run(pool, "pool", {"start": start, "mod0": modulate, "na": na, "fetch0": fetch, "mod1": modulate, "keep0": keep,
                               "dnP": dn, "dn0": dn, "fetchA": fetch, "keep1": keep, "dn1": dn, "dnE": dn,
                               "fetchB": fetch})

    return steps



def tiles(w):
    k, c = w.shape
    return w.reshape(k // (HALF_K * P), HALF_K, P, c // P, P).transpose(3, 0, 2, 1, 4).reshape(c // P, -1, P, HALF)


def columns(v):
    return np.moveaxis(v.reshape(v.shape[:-1] + (v.shape[-1] // P, P)), -1, 0)


def layouts(a):
    ada = [tiles(a["ada_w"][layer]) for layer in range(2)]
    na_in, na_out = tiles(a["na_w_in"][0]), tiles(a["na_w_out"][0])
    dn_in = tiles(a["dn_w_in"][0])
    late = np.concatenate([ada[0][2 * KT:], ada[1]])
    flat = lambda t: t.reshape(-1, P, HALF)
    stream = [flat(ada[0][:2 * KT])]
    for h in range(NA_HEADS):
        stream += [flat(na_in[[h, KT + h, 2 * KT + h, 3 * KT + h]])]
    stream += [flat(na_out), flat(dn_in[6 * KT:])]
    head = lambda h: flat(dn_in[[h, KT + h, 2 * KT + 2 * h, 2 * KT + 2 * h + 1, 4 * KT + 2 * h, 4 * KT + 2 * h + 1]])
    order = [2 * (GROUP - 1 - k // 2) + k % 2 for k in range(KT)]
    w_out = a["dn_w_out"][0].reshape(2, KT, P, D_MODEL)
    stream += [head(h) for h in range(GROUP + 1)] + [flat(tiles(w_out[0, order].reshape(-1, D_MODEL)))]
    stream += [head(h) for h in range(GROUP + 1, DN_K_HEADS)] + [flat(tiles(w_out[1].reshape(-1, D_MODEL)))]
    x = np.concatenate([a["x_prompt"][0], a["x_sample"][0]])
    rpb = np.zeros((NA_HEADS, 2 * ROWS - 1, BIAS_W), np.float32)
    at = GRID_W - WIN_C
    rpb[:, :, at:at + 2 * WIN_C - 1] = a["na_rpb"][0][:, WIN_R - ROWS:WIN_R + ROWS - 1]
    rpb = np.tile(rpb, (1, 1, GRID_W))
    conv = a["dn_conv_w"][0].reshape(CONV, 4 * KT, P)
    heads = np.array([[h, KT + h, 2 * KT + 2 * h, 2 * KT + 2 * h + 1] for h in range(DN_K_HEADS)])
    state = a["state_dn"][0, 0].reshape(2, DN_K_HEADS, 2, P, P)
    alog_dt = np.zeros((P, 2), np.float32)
    alog_dt[64:, 0] = a["dn_a_log"][0].reshape(-1)
    alog_dt[64:, 1] = a["dn_dt_bias"][0].reshape(-1)
    return {
        "stream": np.concatenate(stream),
        "late": flat(late),
        "consts": shape_constants().reshape(P, len(CONSTS), P),
        "cond": columns(np.stack([a["c_ctx"], a["c"][0]])).transpose(0, 2, 1),
        "ada_b": columns(a["ada_b"]).reshape(P, -1),
        "norm_w": columns(np.concatenate([a["norm_w"], a["final_norm_w"][None]])),
        "x": columns(x).transpose(0, 2, 1),
        "cache_k": a["cache_na_k"][0, 0].transpose(2, 1, 0),
        "cache_v": a["cache_na_v"][0, 0],
        "rpb": rpb,
        "conv_w": conv[:, heads].transpose(3, 1, 2, 0),
        "alog_dt": alog_dt,
        "dn_norm_w": a["dn_norm_w"][0][:, None],
        "state": state.transpose(1, 3, 0, 2, 4).reshape(DN_K_HEADS, P, 4, P),
    }


OUTS = {"y_out": (P, KT, T), "k_out": (NA_HEADS, P, CTX), "v_out": (NA_HEADS, P, CTX),
        "state_out": (DN_K_HEADS, P, 4, P)}


def build(nc, shapes):
    def declare(nc):
        dram = {n: nc.dram_tensor(f"in_{n}", shape, F32, kind="ExternalInput").ap() for n, shape in shapes.items()}
        dram |= {n: nc.dram_tensor(f"out_{n}", shape, F32, kind="ExternalOutput").ap() for n, shape in OUTS.items()}
        dram["x_kept"] = nc.dram_tensor("x_kept", (P, KT, T), F32).ap()
        return dram
    listed = type(nc)("TRN2", target_bir_lowering=False, num_devices=1)
    known = emit(listed, None, declare(listed))
    emit(nc, known, declare(nc))


def kernel(**inputs):
    import concourse.bacc as bacc
    from concourse.bass_utils import run_bass_kernel_spmd

    arrays = {n: np.ascontiguousarray(v) for n, v in layouts({k: np.asarray(v) for k, v in inputs.items()}).items()}
    nc = bacc.Bacc("TRN2", target_bir_lowering=False, num_devices=1)
    build(nc, {n: v.shape for n, v in arrays.items()})
    got = run_bass_kernel_spmd(nc, [{f"in_{n}": v for n, v in arrays.items()}], core_ids=[0]).results[0]
    y = got["out_y_out"].transpose(2, 1, 0).reshape(T, D_MODEL)
    state = got["out_state_out"].reshape(DN_K_HEADS, P, 2, 2, P).transpose(2, 0, 3, 1, 4)
    return (np.ascontiguousarray(y[None, :CTX]), np.ascontiguousarray(y[None, CTX:]),
            np.ascontiguousarray(got["out_k_out"].transpose(2, 0, 1)[None, None]),
            np.ascontiguousarray(got["out_v_out"].transpose(2, 0, 1)[None, None]),
            np.ascontiguousarray(state.reshape(1, 1, 2, DN_V_HEADS, P, P)))
```

```python
from contextlib import ExitStack

import concourse.bass as bass
import numpy as np
from concourse import mybir

F32 = mybir.dt.float32
F32R = mybir.dt.float32r
ACT = mybir.ActivationFunctionType
ALU = mybir.AluOpType
AX_X = mybir.AxisListType.X

P = 128
D_MODEL = 2048
KT = D_MODEL // P
CTX = 128
LAT = 256
T = CTX + LAT
CHUNKS = T // P
ROWS, GRID_W = 4, 64
WIN_R, WIN_C = 8, 16
BIAS_W = 2 * GRID_W - 1
NA_HEADS = 16
DN_K_HEADS = 16
DN_V_HEADS = 32
HALF_K = KT // 2
HALF = HALF_K * P
RAW_SLOTS = 4
SPLIT_SLOTS = 4
LOOKAHEAD = 3
CONV = 5
PAD = CONV // 2
LAT_AT = CTX + 2 * PAD
PADDED = T + 3 * PAD
CONV_OUT = PADDED - 2 * PAD
EPS = 1e-6
MASKED = -1e30
SCALE = float(P) ** -0.5
GROUP = 8
CREDIT = 1000
SMALL_LOADS = 8
FILL = 8

CONSTS = ["ident", "ones", "lt", "gt", "le", "ge", "near", "grid"]


def shape_constants():
    m, i = np.arange(P)[:, None], np.arange(P)[None, :]
    grid = np.zeros((P, P), np.float32)
    col, key = np.arange(P)[:, None] % GRID_W, np.arange(GRID_W)[None, :]
    first = np.clip(col - WIN_C // 2, 0, GRID_W - WIN_C)
    grid[:, :GRID_W] = np.where((key >= first) & (key < first + WIN_C), 0.0, MASKED)
    tables = {"ident": m == i, "ones": m >= 0, "le": m <= i, "ge": m >= i, "gt": m > i, "lt": m < i,
              "near": m // 16 == i // 16, "grid": grid}
    return np.concatenate([np.broadcast_to(tables[n], (P, P)).astype(np.float32) for n in CONSTS], axis=1)


class Steps:

    def __init__(self, known=None):
        self.known, self.order, self.turns, self.phase = known, {}, {}, None
        self.sems = {}

    def enter(self, phase, turns):
        self.phase, self.turns[phase] = phase, turns

    def done(self, engine, name, instruction):
        names = self.order.setdefault((self.phase, engine), [])
        if name not in names:
            names.append(name)
        return instruction.then_inc(self.sems[engine], 1)

    def base(self, engine, phase):
        total = CREDIT
        for p, turns in self.known.turns.items():
            if p == phase:
                break
            total += turns * len(self.known.order.get((p, engine), []))
        return total

    def per_turn(self, engine):
        return len(self.known.order.get((self.phase, engine), [])) if self.known else 0

    def count(self, engine, name):
        if self.known is None:
            return CREDIT
        if name not in self.known.order.get((self.phase, engine), []):
            return None
        return self.base(engine, self.phase) + self.known.order[self.phase, engine].index(name) + 1



def plan_fill(items, halves):
    parts = [("part", k, f) for k in halves for f in range(FILL)]
    plan, used = [], 0
    for n, item in enumerate(items):
        want = (n + 1) * len(parts) // (len(items) + 1)
        plan += parts[used:want] + [item]
        used = want
    return plan + parts[used:]


ADA_GROUPS = 2
ADA_HALVES = ([(e, t, half) for pair in range(3) for half in range(2) for e, t in (("dve", pair), ("pe", pair))]
              + [("dve", t, half) for t in (3, 4) for half in range(2)])
ADA_TILES = {"dve": 5, "pe": 3}
assert [h[0] for h in ADA_HALVES[-5::4]] == ["pe", "dve"]
LATE_TILES = 4


def with_ada(halves):
    plan = []
    for k in halves:
        plan += plan_fill([], [k]) + [("ada", k)]
    return plan


NA_PLAN = (with_ada([0, 1, 2, 3, 4]) + [("scores",)] + with_ada([5, 6]) + [("values",)]
           + plan_fill([("turn_probs",), ("ada", 7)], [7]) + [("attend",)])

NEWTON = 3
INVERT = [["ct"], ["p2", "p2t"], ["p4", "p4t", "x1"], ["p8t", "x2"], ["x3"], ["xt0"]]
for _n in range(1, NEWTON + 1):
    INVERT += [[f"t{_n}"], [f"xn{_n}", f"xt{_n}"]]
INVERT += [["res"], ["xf"]]
READ_BY_SCALAR = {"p2", "p2t", "p4", "p4t", "p8t", "xt0"} | {f"x{a}{n}" for a in "nt" for n in range(1, NEWTON + 1)}

_chain = [(5, ("norms",)), (2.5, ("decay", 0)), (2, ("decay", 1)), (1.5, ("broad", 1)), (0, ("unit",)), (2, ("decay", 2)),
          (1.5, ("broad", 2)), (1, ("gram", 0)), (2, ("gram", 1)), (2, ("gram", 2)), (1, ("values", 0)),
          (1, ("values", 1))]
for _stage in range(len(INVERT) - 1):
    _chain += [(3 if _stage < 2 and c < 2 - _stage else 2 if _stage < 2 else 1, ("invert", _stage, c)) for c in range(CHUNKS)]
_chain += [(1, ("recall", "A"))] + [(1, ("invert", len(INVERT) - 1, c)) for c in range(CHUNKS)]
_chain += [(4, ("apply", "0")), (0, ("apply", "A")), (3, ("state", "A")), (0, ("state", "0")), (3, ("recall", "B")),
           (3, ("apply", "B")), (3, ("out",)), (0, ("squares",)), (2, ("out_norm",))]


def merge(chain, parts):
    total = sum(weight for weight, _ in chain)
    plan, seen, used = [], 0, 0
    for weight, item in chain:
        seen += weight
        want = int(seen * len(parts) / (total + 2))
        plan += parts[used:want] + [item]
        used = want
    return plan + parts[used:]


TAPS_AT = 4 * FILL
DN_PARTS = [("part", k, f) for k in range(12) for f in range(FILL)]
DN_CHAIN = [item for _, item in _chain]
DN_PLAN = merge(_chain, DN_PARTS)
DN_PLANS = {"dnP": DN_PARTS + [("squares",), ("gates",)], "dn0": DN_PLAN + [("gates",)], "dn1": DN_PLAN + [("gates",)],
            "dnE": DN_CHAIN}


INVERT_OPERANDS = {"p2": ("e", "d"), "p2t": ("d", "e"), "p4": ("g", "f"), "p4t": ("f", "g"), "x1": ("g", "x"),
                   "p8t": ("d", "e"), "x2": ("e", "x"), "x3": ("f", "x"), "t": ("mtr", "x"), "xn": ("g", "d"),
                   "xt": ("d", "g"), "xf": ("g", "d")}
INVERT_NEEDS = {"ct": [("dve", "c")], "p2": [("pool", "near"), ("dve", "near")], "p2t": [],
                "p4": [("act", "p2t_")], "p4t": [], "x1": [("pool", "x0")],
                "p8t": [("act", "p4t_")], "x2": [("dve", "x1_")], "x3": [("act", "p8t_"), ("dve", "x2_")],
                "xt0": [("dve", "x3_")], "res": [("act", f"xt{NEWTON}_")], "xf": [("dve", "res_")]}
for _n in range(1, NEWTON + 1):
    INVERT_NEEDS |= {f"t{_n}": [("act", f"xt{_n - 1}_"), ("act", "mtr")], f"xn{_n}": [("dve", f"t{_n}_")],
                     f"xt{_n}": []}


def dn_products():
    made = []
    for item in DN_CHAIN:
        what, arg = item[0], item[1] if len(item) > 1 else None
        if what == "decay":
            made.append((f"decay{arg}", "act"))
        elif what == "broad":
            made.append((f"broad{arg}", "act"))
        elif what == "norms":
            made += [("ss0", "act"), ("ss1", "act")]
        elif what == "gram":
            made.append((f"gram{arg}", "act"))
        elif what == "values":
            made.append((f"values{arg}", "act"))
        elif what == "invert":
            made += [(f"{p}_{item[2]}", "act" if p in READ_BY_SCALAR else "dve") for p in INVERT[arg]]
        elif what in ("recall", "apply"):
            made.append((f"{what}{arg}", "act" if what == "apply" and arg == "B" else "dve"))
        elif what == "state":
            made.append((f"state{arg}", "act" if arg == "0" else "dve"))
        elif what == "out_norm":
            made += [("on0", "act"), ("on1", "act")]
    return made


PRODUCTS = dn_products()
PRODUCT_AT = {name: n for n, (name, _) in enumerate(PRODUCTS)}
RING, RING_AT = 4, 2
assert len(PRODUCTS) % RING == 0
SCAN = {"0": (0, 0), "A": (1, 2), "B": (2, 1)}


def emit(nc, known, dram):
    steps = Steps(known)
    done = steps.done

    with ExitStack() as ctx:
        def sb(name, shape, dt=F32):
            return ctx.enter_context(nc.sbuf_tensor(name, shape, dt))

        def sem(name):
            return ctx.enter_context(nc.semaphore(name))

        banks = [ctx.enter_context(nc.psum_tensor(f"bank{n}", [P, 512], F32)) for n in range(8)]

        raw = sb("raw", [P, RAW_SLOTS, HALF])
        w_hi = sb("w_hi", [P, SPLIT_SLOTS, HALF], F32R)
        w_lo = sb("w_lo", [P, SPLIT_SLOTS, HALF], F32R)
        h_hi = sb("h_hi", [P, KT, T], F32R)
        h_lo = sb("h_lo", [P, KT, T], F32R)
        y = sb("y", [P, KT + 2, T])
        consts = sb("consts", [P, len(CONSTS), P])
        K = {n: consts[:, j, :] for j, n in enumerate(CONSTS)}
        mods = sb("mods", [P, 2 * 3 * KT, 2])
        ada_b = sb("ada_b", [P, 2 * 3 * KT])
        cond = sb("cond", [P, KT, 2])
        norm_w = sb("norm_w", [P, 3, KT])
        gain = sb("gain", [P, KT, 2])
        bias_eps = sb("bias_eps", [P, 2])
        twice = sb("twice", [P, P])
        conv_w = sb("conv_w", [P, DN_K_HEADS, 4, CONV])
        alog_dt = sb("alog_dt", [P, 3])
        dn_norm_w = sb("dn_norm_w", [P, 1])
        ada_terms = sb("ada_terms", [P, HALF])
        n = CHUNKS * 2 * DN_V_HEADS
        neg_egc, beta_egl, egl = (ada_terms[:, j * n:(j + 1) * n].rearrange("p (c d h) -> p c d h", c=CHUNKS, d=2)
                                  for j in range(3))
        bg = ada_terms[:, 3 * n:3 * n + CHUNKS * P].rearrange("p (c h) -> p c h", c=CHUNKS)
        beta_now = sb("beta_now", [P, CHUNKS, 2, 2])
        g_now = sb("g_now", [P, CHUNKS, 2, 2])

        scratch_at = (nc.sbuf_base + 63) // 64 * 64
        scratch_end = nc.sbuf_usable_end

        class Region:
            def __init__(self, at=0):
                self.at = scratch_at + at

            def take(self, name, shape, dt=F32):
                size = 4 * int(np.prod(shape[1:]))
                t = nc.alloc_sbuf_tensor_at(name, shape, dt, offset=self.at)
                self.at += (size + 31) // 32 * 32
                assert self.at <= scratch_end, (name, self.at - scratch_end)
                return t

        region = Region()
        x = y[:, 2:KT + 2, :]
        y_hi = region.take("y_hi", [P, KT, T], F32R)
        y_lo = region.take("y_lo", [P, KT, T], F32R)
        rstd = region.take("rstd", [P, T])
        logs = region.take("logs", [P, T])
        squares = region.take("squares", [P, 2, T])
        scaled = region.take("scaled", [P, 2, T])
        shifted = region.take("shifted", [P, 2, T])
        square_sum = shifted[:, 0, :]
        region = Region()
        bias = region.take("bias", [P, 2, NA_HEADS, ROWS * GRID_W])
        cond_rows = region.take("cond_rows", [P, 2, D_MODEL])
        qk = region.take("qk", [P, 2, T])
        vT = region.take("vT", [P, T])
        V = region.take("V", [P, CHUNKS, P])
        gate_na = region.take("gate_na", [P, T])
        cache_k1 = region.take("cache_k1", [P, P])
        cache_v1 = region.take("cache_v1", [P, P])
        probs = region.take("probs", [P, CTX + 2 * T])
        raw_ada = region.take("raw_ada", [P, 2, HALF])
        probsT = region.take("probsT", [P, CTX + CHUNKS * LAT])
        ada_sums = region.take("ada_sums", [P, ADA_GROUPS, ADA_TILES["dve"], 2, 2])
        stats = region.take("stats", [P, 3, 3])
        region = Region()
        inv = {}
        f32r_at = region.at
        for c in range(CHUNKS):
            for name in ("d", "e", "f", "g", "x"):
                inv[name, c] = region.take(f"inv_{name}{c}", [P, 4, P], F32R)
        overlay = Region(f32r_at - scratch_at)
        vn = {s: overlay.take(f"v_new{s}", [P, 4, P]) for s in "0AB"}
        vs = {s: overlay.take(f"v_state{s}", [P, 4, P]) for s in "0A"}
        s_out = overlay.take("s_out", [P, 4, P])
        o_sq = overlay.take("o_sq", [P, 2, T])
        o_rs = overlay.take("o_rs", [P, 2, T])
        o_n = overlay.take("o_n", [P, 2, T])
        qk_sq = overlay.take("qk_sq", [P, 2, CONV_OUT])
        qk_rs = overlay.take("qk_rs", [P, 2, CONV_OUT])
        assert overlay.at <= region.at
        for c in range(CHUNKS):
            inv["mtr", c] = Region(region.at - scratch_at).take(f"inv_mtr{c}", [P, 4, P], F32R)
            for name in ("c", "mt"):
                inv[name, c] = region.take(f"inv_{name}{c}", [P, 4, P])
        R = {"A": inv["mt", 1], "B": inv["mt", 2]}
        dn_qk = region.take("dn_qk", [P, 2, T])
        padded = region.take("padded", [P, 2, PADDED])
        dn_v = region.take("dn_v", [P, CHUNKS, 2, P])
        k_nat = region.take("k_nat", [P, CHUNKS, P])
        gram = region.take("gram", [P, 2, 2, P])
        decay = [region.take(f"decay{c}", [P, 4, P]) for c in range(CHUNKS)]
        q_dec = [None] + [region.take(f"q_dec{c}", [P, 4, P]) for c in (1, 2)]
        S = region.take("S", [P, 4, P])
        conv = region.take("conv", [P, 4, CONV_OUT])
        g_mask = [inv["c", c] for c in range(CHUNKS)]
        overlay = Region(f32r_at - scratch_at)
        bgT = overlay.take("bgT", [P, T])
        bt = overlay.take("bt", [P, T])
        bt2 = overlay.take("bt2", [P, T])

        s = {n: sem(n) for n in ("tensor_steps", "scalar_steps", "vector_steps", "pool_steps", "hi_ready",
                                 "halves_done", "evacuated", "small_in", "x_in", "x_out", "bias_in", "k_out",
                                 "pool_waits", "v_out", "cache_k_in", "cache_v_in", "x0_in", "state_in", "state_out", "y_out")}
        steps.sems = {"pe": s["tensor_steps"], "act": s["scalar_steps"], "dve": s["vector_steps"],
                      "pool": s["pool_steps"]}
        ada_full = [sem(f"ada_full{n}") for n in range(2)]
        ada_used = [sem(f"ada_used{n}") for n in range(2)]
        raw_full = [sem(f"raw_full{n}") for n in range(RAW_SLOTS)]
        consumed = [sem(f"consumed{n}") for n in range(RAW_SLOTS)]

        pos = {}
        n0 = m0 = t0 = 0
        for phase, turns, split, plain in (("ada", 4 // ADA_GROUPS, 0, 16 * ADA_GROUPS), ("na", NA_HEADS, 8, 0), ("out0", KT // 2, 4, 0),
                                           ("ba", 1, 2, 0), ("dnP", 1, 12, 0), ("dn0", GROUP, 12, 0),
                                           ("outA", KT // 2, 4, 0), ("dn1", GROUP - 1, 12, 0), ("outB", KT // 2, 4, 0)):
            pos[phase] = (n0, m0, split + plain, split, t0, split // 2)
            n0, m0, t0 = n0 + turns * (split + plain), m0 + turns * split, t0 + turns * split // 2
        N_HALVES = n0
        assert N_HALVES == dram["stream"].shape[0], (N_HALVES, dram["stream"].shape)

        def raw_wait(eng, phase, turn, k):
            n, _, per, _, _, _ = pos[phase]
            eng.wait_ge(raw_full[(n + k) % RAW_SLOTS], 16 * ((n + k) // RAW_SLOTS + 1) + turn * (16 * per // RAW_SLOTS))
            return (n + k) % RAW_SLOTS

        def split_place(phase, turn, k):
            n, m, per, split, _, _ = pos[phase]
            ahead, kk = divmod(k, split)
            if phase == "ba":
                ahead, kk = 0, k
            raw_n = n + ahead * per + kk
            return raw_n, m + k

        def split_hi(act, phase, turn, k):
            raw_n, mk = split_place(phase, turn, k)
            _, _, per, split, _, _ = pos[phase]
            act.wait_ge(raw_full[raw_n % RAW_SLOTS], 16 * (raw_n // RAW_SLOTS + 1) + turn * (16 * per // RAW_SLOTS))
            if mk >= SPLIT_SLOTS:
                act.wait_ge(s["halves_done"], mk - SPLIT_SLOTS + 1 + turn * split)
            nc.scalar.activation(w_hi[:, mk % SPLIT_SLOTS, :], raw[:, raw_n % RAW_SLOTS, :], ACT.Copy)\
                .then_inc(s["hi_ready"], 1)

        def split_lo(dve, phase, turn, k):
            raw_n, mk = split_place(phase, turn, k)
            split = pos[phase][3]
            dve.wait_ge(s["hi_ready"], mk + 1 + turn * split)
            nc.vector.tensor_tensor(w_lo[:, mk % SPLIT_SLOTS, :], raw[:, raw_n % RAW_SLOTS, :],
                                    w_hi[:, mk % SPLIT_SLOTS, :].bitcast(F32), ALU.subtract)\
                .then_inc(consumed[raw_n % RAW_SLOTS], 1)

        def operands_ready(pe, phase, k, part):
            made = FIRST_USE.get(phase)
            kt, chunk = k * HALF_K + part, 1 if made in ("mod0", "mod1") else 4
            if made is None or k >= 2 or kt % chunk:
                return
            name = f"lo{kt}" if chunk == 1 else f"y_lo{kt}"
            if known is not None:
                pe.wait_ge(steps.sems["dve"], steps.base("dve", made) + known.order[made, "dve"].index(name) + 1)

        def multiply(pe, phase, turn, k, part, hi, lo):
            raw_n, mk = split_place(phase, turn, k)
            _, m, per, split, t, tiles = pos[phase]
            tile, half = k // 2, k % 2
            bank = banks[(t + tile) % 2]
            if part == 0:
                pe.wait_ge(consumed[raw_n % RAW_SLOTS], raw_n // RAW_SLOTS + 2 + turn * (per // RAW_SLOTS))
                if half == 0:
                    pe.wait_ge(s["evacuated"], t + tile + 1 + turn * tiles)
            operands_ready(pe, phase, k, part)
            each = HALF_K // FILL
            for j in range(part * each, (part + 1) * each):
                kt = half * HALF_K + j
                w = slice(j * P, (j + 1) * P)
                slot = mk % SPLIT_SLOTS
                nc.tensor.matmul(bank[:, 0:T], w_hi[:, slot, w], hi[:, kt, :], start=kt == 0, stop=False)
                nc.tensor.matmul(bank[:, 0:T], w_hi[:, slot, w], lo[:, kt, :], start=False, stop=False)
                last = nc.tensor.matmul(bank[:, 0:T], w_lo[:, slot, w], hi[:, kt, :], start=False, stop=kt == KT - 1)
            if part == FILL - 1:
                last.then_inc(s["halves_done"], 1)

        def tile_done(eng, phase, turn, tile):
            _, m, _, split, t, _ = pos[phase]
            eng.wait_ge(s["halves_done"], m + 2 * tile + 2 + turn * split)
            return banks[(t + tile) % 2]

        def tile_read(eng, phase, turn, tile):
            _, _, _, _, t, tiles = pos[phase]
            eng.wait_ge(s["evacuated"], t + tile + 3 + turn * tiles)

        def y_row(n):
            return y[:, bass.ds(n, 1), :].rearrange("p a t -> p (a t)")

        def half_used(eng, phase, turn, k):
            n, _, per, _, _, _ = pos[phase]
            eng.wait_ge(consumed[(n + k) % RAW_SLOTS], (n + k) // RAW_SLOTS + 2 + turn * (per // RAW_SLOTS))

        def heads(phase, turn):
            if phase == "dnP":
                return None, 0, None, KT
            if phase == "dn0":
                return turn, turn + 1, turn * -2 + KT, turn * -2 + (KT - 2)
            if phase == "dn1":
                return turn + GROUP, turn + (GROUP + 1), turn * 2, turn * 2 + 2
            return 2 * GROUP - 1, None, KT - 2, None

        def barrier(eng, me, phase):
            names = [p for p, _ in PHASES]
            tiles = sum(turns * pos[p][5] for p, turns in PHASES[:names.index(phase)] if p in pos)
            if tiles:
                eng.wait_ge(s["evacuated"], tiles + 2)
            for other in ("pe", "act", "dve", "pool"):
                if known is not None:
                    since = {"ada": "squares0", "norm0": "ada"}.get(phase, FIRST_USE.get(phase, phase) if me == "pe" else phase)
                    eng.wait_ge(steps.sems[other], steps.base(other, since))

        def ring(name):
            return banks[RING_AT + PRODUCT_AT[name] % RING]

        def ring_free(name):
            n = PRODUCT_AT[name] - RING
            before, reader = PRODUCTS[n]
            return reader, "v_newB" if before == "applyB" else before, n < 0

        def wait_steps(eng, turn, *which):
            latest = {}
            for engine, name, *back in which:
                at = steps.count(engine, name)
                if at is None:
                    continue
                at -= steps.per_turn(engine) if back and back[0] else 0
                latest[engine] = max(at, latest.get(engine, 0))
            for engine, at in latest.items():
                eng.wait_ge(steps.sems[engine], at + turn * steps.per_turn(engine) if steps.known else CREDIT)

        FIRST_USE = {"na": "mod0", "out0": "ysplit0", "ba": "mod1", "outA": "ysplitA", "outB": "ysplitB"}
        PHASES = [("start", 1), ("squares0", 1), ("ada", 4 // ADA_GROUPS), ("norm0", 1), ("mod0", 1), ("na", NA_HEADS), ("ysplit0", 1), ("fetch0", 1), ("out0", KT // 2),
                  ("norm1", 1), ("mod1", 1), ("ba", 1), ("keep0", 1), ("dnP", 1), ("dn0", GROUP),
                  ("ysplitA", 1), ("fetchA", 1), ("outA", KT // 2), ("keep1", 1), ("dn1", GROUP - 1), ("dnE", 1), ("ysplitB", 1),
                  ("fetchB", 1), ("outB", KT // 2), ("norm2", 1), ("final", 1)]

        def run(eng, me, parts):
            for phase, turns in PHASES:
                steps.enter(phase, turns)
                body = parts.get(phase)
                if body is None:
                    continue
                barrier(eng, me, phase)
                if turns == 1:
                    body(eng, phase, 0)
                elif phase == "outB":
                    with eng.Fori(0, turns - 1) as turn:
                        body(eng, phase, turn)
                    body(eng, phase, turns - 1, last=True)
                else:
                    with eng.Fori(0, turns) as turn:
                        body(eng, phase, turn)

        block = ctx.enter_context(nc.Block())

        @block.sync
        def _(sp):
            def load(n, slot, turn):
                sp.wait_ge(consumed[slot], turn + 1)
                sp.dma_start(raw[:, slot, :], dram["stream"][bass.ds(n, 1)].rearrange("a p f -> p (a f)"))\
                    .then_inc(raw_full[slot], 16)

            with sp.Fori(0, N_HALVES // RAW_SLOTS) as turn:
                for slot in range(RAW_SLOTS):
                    load(RAW_SLOTS * turn + slot, slot, turn)
            for slot in range(N_HALVES % RAW_SLOTS):
                load(N_HALVES // RAW_SLOTS * RAW_SLOTS + slot, slot, N_HALVES // RAW_SLOTS)

        @block.tensor
        def _(pe):
            pe.sem_inc(s["tensor_steps"], CREDIT)
            for n in range(2):
                pe.sem_inc(ada_used[n], 1)

            def sum_squares(pe, phase, turn):
                done("pe", "total", nc.tensor.matmul(banks[2][:, 0:T], K["ones"], square_sum, start=True, stop=True))

            def ada_half(bank, weights, tile, half):
                for j in range(HALF_K):
                    kt = half * HALF_K + j
                    mm = nc.tensor.matmul(bank[:, 2 * tile:2 * tile + 2], weights[:, j * P:(j + 1) * P],
                                          cond[:, kt, :], start=kt == 0, stop=kt == KT - 1)
                return mm

            def ada(pe, phase, turn):
                for g in range(ADA_GROUPS):
                    wait_steps(pe, turn, ("dve", f"mods{g}", True))
                    for k, (engine, tile, half) in enumerate(ADA_HALVES):
                        if engine == "pe":
                            slot = raw_wait(pe, phase, turn, 16 * g + k)
                            ada_half(banks[4 + g], raw[:, slot, :], tile, half).then_inc(consumed[slot], 1)

            def na(pe, phase, turn):
                for item in NA_PLAN:
                    if item[0] == "part":
                        multiply(pe, phase, turn, item[1], item[2], h_hi, h_lo)
                    elif item[0] == "scores":
                        tile_read(pe, phase, turn, 1)
                        pe.wait_ge(s["cache_k_in"], 16 * (turn + 1))
                        wait_steps(pe, turn, ("dve", "y", 1))
                        mm = nc.tensor.matmul(banks[2][:, 0:CTX], qk[:, 0, 0:CTX], qk[:, 1, 0:CTX], start=True, stop=True)
                        done("pe", "scores0", mm)
                        for r in range(2):
                            q = qk[:, 0, CTX + r * P:CTX + (r + 1) * P]
                            nc.tensor.matmul(banks[3 + r][:, 0:LAT], q, qk[:, 1, CTX:T], start=True, stop=True)
                            mm = nc.tensor.matmul(banks[3 + r][:, LAT:T], q, cache_k1[:], start=True, stop=True)
                            done("pe", f"scores{r + 1}", mm)
                    elif item[0] == "values":
                        tile_read(pe, phase, turn, 2)
                        wait_steps(pe, turn, ("act", "V", 1))
                        for c in range(CHUNKS):
                            mm = nc.tensor.transpose(banks[5][:, c * P:(c + 1) * P], vT[:, c * P:(c + 1) * P], K["ident"])
                        done("pe", "values", mm)
                    elif item[0] == "turn_probs":
                        wait_steps(pe, turn, ("pool", "probs2"), ("dve", "probsT0", 1))
                        nc.tensor.transpose(banks[6][:, 0:P], probs[:, 0:P], K["ident"])

                        def turned(bank, at, c):
                            for r in range(2):
                                src = probs[:, CTX + r * T + c * P:CTX + r * T + (c + 1) * P]
                                mm = nc.tensor.transpose(bank[:, at + r * P:at + (r + 1) * P], src, K["ident"])
                            return mm
                        done("pe", "probsT0", turned(banks[6], P, 0))
                        turned(banks[2], 0, 1)
                        done("pe", "probsT1", turned(banks[2], LAT, 2))
                    elif item[0] == "attend":
                        wait_steps(pe, turn, ("dve", "probsT1"), ("act", "V"))
                        pe.wait_ge(s["cache_v_in"], 16 * (turn + 1))
                        nc.tensor.matmul(banks[3][:, 0:CTX], V[:, 0, :], probsT[:, 0:CTX], start=True, stop=True)
                        for c, values in enumerate((V[:, 1, :], V[:, 2, :], cache_v1[:])):
                            mm = nc.tensor.matmul(banks[3][:, CTX:T], values,
                                                  probsT[:, CTX + c * LAT:CTX + (c + 1) * LAT], start=c == 0,
                                                  stop=c == 2)
                        done("pe", "attend", mm)

            def out(pe, phase, turn, last=False):
                for k in range(4):
                    for part in range(FILL):
                        multiply(pe, phase, turn, k, part, y_hi, y_lo)

            def ba(pe, phase, turn):
                for k in range(2):
                    for part in range(FILL):
                        multiply(pe, phase, turn, k, part, h_hi, h_lo)
                wait_steps(pe, turn, ("dve", "g"))
                for c in range(CHUNKS):
                    mm = nc.tensor.transpose(banks[2][:, c * P:(c + 1) * P], bgT[:, c * P:(c + 1) * P], K["ident"])
                done("pe", "bg", mm)
                wait_steps(pe, turn, ("dve", "bg"))
                for n, masks in enumerate((("le", "ge"), ("gt", "lt"), ("ones", "ones"))):
                    for c in range(CHUNKS):
                        for d in range(2):
                            at = (c * 2 + d) * DN_V_HEADS
                            mm = nc.tensor.matmul(banks[3 + n][:, at:at + DN_V_HEADS], K[masks[d]],
                                                  bg[:, c, 64 + 32 * d:96 + 32 * d], start=True, stop=True)
                    done("pe", f"sums{n}", mm)

            def dn(pe, phase, turn):
                for item in DN_PLANS[phase]:
                    what, arg = item[0], item[1] if len(item) > 1 else None
                    if what == "part":
                        multiply(pe, phase, turn, arg, item[2], h_hi, h_lo)
                    elif what == "decay":
                        wait_steps(pe, turn, ("pool", f"g_mask{arg}", True), ring_free(f"decay{arg}"))
                        for d, mask in enumerate(("gt", "lt")):
                            mm = nc.tensor.matmul(ring(f"decay{arg}")[:, 2 * d * P:(2 * d + 2) * P], K[mask],
                                                  g_mask[arg][:, 2 * d:2 * d + 2, :].rearrange("p v i -> p (v i)"),
                                                  start=True, stop=True)
                        done("pe", f"decay{arg}", mm)
                    elif what == "broad":
                        wait_steps(pe, turn, ring_free(f"broad{arg}"))
                        mm = nc.tensor.matmul(ring(f"broad{arg}")[:], K["ones"],
                                              g_mask[arg][:].rearrange("p v i -> p (v i)"), start=True, stop=True)
                        done("pe", f"broad{arg}", mm)
                    elif what == "norms":
                        for n in range(2):
                            wait_steps(pe, turn, ("pool", f"square{n}", True), ring_free(f"ss{n}"))
                            mm = nc.tensor.matmul(ring(f"ss{n}")[:, 0:CONV_OUT], K["ones"], qk_sq[:, n, :], start=True, stop=True)
                            done("pe", f"ss{n}", mm)
                    elif what == "gram":
                        c = arg
                        wait_steps(pe, turn, ring_free(f"gram{c}"), ("dve", "unit1"))
                        kT = dn_qk[:, 1, c * P:(c + 1) * P]
                        bank = ring(f"gram{c}")
                        nc.tensor.matmul(bank[:, 0:P], kT, kT, start=True, stop=True)
                        nc.tensor.matmul(bank[:, P:2 * P], kT, dn_qk[:, 0, c * P:(c + 1) * P], start=True, stop=True)
                        mm = nc.tensor.transpose(bank[:, 2 * P:3 * P], kT, K["ident"])
                        done("pe", f"gram{c}", mm)
                    elif what == "values":
                        wait_steps(pe, turn, ring_free(f"values{arg}"), ("act", f"conv{2 + arg}", True))
                        for c in range(CHUNKS):
                            at = c * P + (PAD if c else 0)
                            mm = nc.tensor.transpose(ring(f"values{arg}")[:, c * P:(c + 1) * P],
                                                     conv[:, 2 + arg, at:at + P], K["ident"])
                        done("pe", f"values{arg}", mm)
                    elif what == "invert":
                        invert(pe, turn, arg, item[2])
                    elif what == "recall":
                        if arg == "B":
                            wait_steps(pe, turn, ring_free("recallB"), ("dve", "stateA"))
                        else:
                            pe.wait_ge(s["state_in"], 16 * (turn + {"dn0": 1, "dn1": GROUP + 1, "dnE": 2 * GROUP}[phase]))
                            wait_steps(pe, turn, ring_free("recallA"))
                        for d in range(2):
                            c = SCAN[arg][d]
                            mm = nc.tensor.matmul(ring(f"recall{arg}")[:, 2 * d * P:(2 * d + 2) * P],
                                                  dn_qk[:, 1, c * P:(c + 1) * P],
                                                  S[:, 2 * d:2 * d + 2, :].rearrange("p v e -> p (v e)"),
                                                  start=True, stop=True)
                        done("pe", f"recall{arg}", mm)
                    elif what == "apply":
                        wait_steps(pe, turn, ring_free(f"apply{arg}"), ("dve", f"xf_{CHUNKS - 1}"),
                                   ("act", "values1") if arg == "0" else ("dve", f"recall{arg}"))
                        for u in range(4):
                            c = SCAN[arg][u // 2]
                            rhs = dn_v[:, 0, u % 2, :] if arg == "0" else R[arg][:, u, :]
                            mm = nc.tensor.matmul(ring(f"apply{arg}")[:, u * P:(u + 1) * P], inv["c", c][:, u, :],
                                                  rhs, start=True, stop=True)
                        done("pe", f"apply{arg}", mm)
                    elif what == "state":
                        if arg == "A":
                            outputs(pe, turn, "A")
                        wait_steps(pe, turn, ring_free(f"state{arg}"), ("dve", f"apply{arg}"))
                        for d in range(2):
                            mm = nc.tensor.matmul(ring(f"state{arg}")[:, 2 * d * P:(2 * d + 2) * P],
                                                  k_nat[:, SCAN[arg][d], :],
                                                  vs[arg][:, 2 * d:2 * d + 2, :].rearrange("p v e -> p (v e)"),
                                                  start=True, stop=True)
                        done("pe", f"state{arg}", mm)
                        if arg == "0":
                            outputs(pe, turn, "0")
                    elif what == "out":
                        outputs(pe, turn, "B")
                    elif what == "out_norm":
                        for v in range(2):
                            wait_steps(pe, turn, ring_free(f"on{v}"), ("act", f"o_sq{v}"))
                            mm = nc.tensor.matmul(ring(f"on{v}")[:, 0:T], K["ones"], o_sq[:, v, :], start=True, stop=True)
                            done("pe", f"on{v}", mm)

            def outputs(pe, turn, step):
                wait_steps(pe, turn, ("act", f"v_new{step}"), ("pool", "q_dec2"), ("dve", "xf_2"),
                           ("dve", "o_n1", True))
                for v in range(2):
                    o = banks[6 + v]
                    for d in range(2):
                        c, u = SCAN[step][d], 2 * d + v
                        mm = nc.tensor.matmul(o[:, c * P:(c + 1) * P], vn[step][:, u, :], decay[c][:, u, :],
                                              start=step == "A" and d == 0, stop=False, skip_group_check=True)
                        if step != "0":
                            mm = nc.tensor.matmul(o[:, c * P:(c + 1) * P], S[:, u, :], q_dec[c][:, u, :],
                                                  start=False, stop=step == "B" and d == 1, skip_group_check=True)
                done("pe", f"out{step}", mm)

            def invert(pe, turn, stage, c):
                g = {n: inv[n, c] for n in ("c", "mt", "mtr", "d", "e", "f", "g", "x")}
                def out_of(name):
                    wait_steps(pe, turn, ring_free(f"{name}_{c}"), *[(e, f"{n}{c}") for e, n in INVERT_NEEDS[name]])
                    return ring(f"{name}_{c}")

                def four(name, lhs, rhs, wide=False):
                    bank = out_of(name)
                    for u in range(4):
                        b = g[rhs][:, u, :]
                        mm = nc.tensor.matmul(bank[:, u * P:(u + 1) * P], g[lhs][:, u, :], b.bitcast(F32) if wide else b,
                                              start=True, stop=True)
                    done("pe", f"{name}_{c}", mm)

                def turned(name, src):
                    bank = out_of(name)
                    for u in range(4):
                        a = g[src][:, u, :]
                        mm = nc.tensor.transpose(bank[:, u * P:(u + 1) * P], a.bitcast(F32) if src == "x" else a, K["ident"])
                    done("pe", f"{name}_{c}", mm)

                for name in INVERT[stage]:
                    if name in ("ct", "xt0"):
                        turned(name, "c" if name == "ct" else "x")
                    elif name == "res":
                        four(name, "mt", "x", wide=True)
                    else:
                        kind = name if name in INVERT_OPERANDS else name.rstrip("0123456789")
                        four(name, *INVERT_OPERANDS[kind])

            run(pe, "pe", {"ada": ada, "norm0": sum_squares, "na": na, "out0": out, "norm1": sum_squares, "ba": ba,
                           "dnP": dn, "dn0": dn, "outA": out, "dn1": dn, "dnE": dn, "outB": out,
                           "norm2": sum_squares})

        @block.scalar
        def _(act):
            act.sem_inc(s["scalar_steps"], CREDIT)
            act.sem_inc(s["evacuated"], 2)

            def squares_of_x(act, phase, turn):
                act.wait_ge(s["x0_in"], 16)
                for k in range(KT):
                    if k >= 2:
                        wait_steps(act, turn, ("pool", f"added{k - 2}"))
                    done("act", f"square{k}", nc.scalar.activation(squares[:, k % 2, :], x[:, k, :], ACT.Square))

            def norm(act, phase, turn):
                wait_steps(act, turn, ("pe", "total"))
                done("act", "log", nc.scalar.activation(logs[:], banks[2][:, 0:T], ACT.Ln, bias=bias_eps[:, 0:1],
                                                        scale=1.0 / D_MODEL))
                wait_steps(act, turn, ("act", "log"))
                done("act", "rstd", nc.scalar.activation(rstd[:], logs[:], ACT.Exp, scale=-0.5))

            def start(act, phase, turn):
                small = [(cond[:], "cond"), (ada_b[:], "ada_b"), (consts[:], "consts"), (norm_w[:], "norm_w"),
                         (conv_w[:], "conv_w"), (alog_dt[:, 0:2], "alog_dt"), (dn_norm_w[:], "dn_norm_w")]
                for dst, name in small:
                    act.dma_start(dst, dram[name]).then_inc(s["small_in"], 16)
                rows = bass.AP(dram["cond_rows"].tensor, 0, [[0, P], [1, 2 * D_MODEL]])
                act.dma_start(cond_rows[:].rearrange("p g k -> p (g k)"), rows).then_inc(s["small_in"], 16)
                act.dma_start(x, dram["x"]).then_inc(s["x0_in"], 16)
                for row in range(ROWS):
                    for keys in range(ROWS):
                        rel = bass.AP(dram["rpb"].tensor, (ROWS - 1 - row + keys) * GRID_W * BIAS_W + GRID_W - 1,
                                      [[BIAS_W - 1, GRID_W], [(2 * ROWS - 1) * GRID_W * BIAS_W, NA_HEADS], [1, GRID_W]])
                        dst = bias[(row % 2) * GRID_W:(row % 2 + 1) * GRID_W, row // 2, :,
                                   keys * GRID_W:(keys + 1) * GRID_W]
                        act.dma_start(dst, rel).then_inc(s["bias_in"], 16)
                act.wait_ge(s["small_in"], 16 * SMALL_LOADS)
                done("act", "cond_rows", nc.scalar.activation(cond_rows[:], cond_rows[:], ACT.Silu))
                done("act", "cond", nc.scalar.activation(cond[:], cond[:], ACT.Silu))

            def modulate(act, phase, turn):
                layer = 0 if phase == "mod0" else 1
                if phase == "mod0":
                    for k in range(LOOKAHEAD):
                        split_hi(act, "na", 0, k)
                wait_steps(act, turn, ("dve", "gain"))
                for k in range(KT):
                    wait_steps(act, turn, (("dve", "pool")[k % 2], f"scaled{k}"))
                    if k >= 2:
                        wait_steps(act, turn, ("dve", f"lo{k - 2}"))
                    for g, sl in ((0, slice(0, CTX)), (1, slice(CTX, T))):
                        i = nc.scalar.activation(shifted[:, k % 2, sl], scaled[:, k % 2, sl], ACT.Identity,
                                                 bias=mods[:, layer * 3 * KT + k, g:g + 1], scale=gain[:, k, g:g + 1])
                    done("act", f"shifted{k}", i)
                    if k % 2 == 0:
                        wait_steps(act, turn, ("act", f"shifted{k}"))
                        done("act", f"hi{k}", nc.scalar.activation(h_hi[:, k, :], shifted[:, k % 2, :], ACT.Copy))

            def na(act, phase, turn):
                for item in NA_PLAN:
                    if item[0] == "part" and item[2] == 0:
                        k = item[1]
                        split_hi(act, phase, turn, k + LOOKAHEAD)
                        if k == 2:
                            bank = tile_done(act, phase, turn, 0)
                            nc.scalar.activation(qk[:, 0, :], bank[:, 0:T], ACT.Copy, scale=SCALE).then_inc(s["evacuated"], 1)
                        elif k == 4:
                            bank = tile_done(act, phase, turn, 1)
                            act.wait_ge(s["cache_k_in"], 16 * (turn + 1))
                            nc.scalar.activation(qk[:, 1, :], bank[:, 0:T], ACT.Copy).then_inc(s["evacuated"], 1)
                        elif k == 6:
                            bank = tile_done(act, phase, turn, 2)
                            act.wait_ge(s["cache_v_in"], 16 * (turn + 1))
                            nc.scalar.activation(vT[:], bank[:, 0:T], ACT.Copy).then_inc(s["evacuated"], 1)
                    elif item[0] == "scores":
                        for r in range(3):
                            wait_steps(act, turn, ("dve", f"max{r}"))
                            wide = slice(0, CTX) if r == 0 else slice(0, T)
                            dst = probs[:, 0:CTX] if r == 0 else probs[:, CTX + (r - 1) * T:CTX + r * T]
                            if r == 0:
                                wait_steps(act, turn, ("pe", "probsT1", 1))
                            done("act", f"exp{r}", nc.scalar.activation(
                                dst, banks[2 + r][:, wide], ACT.Exp, bias=stats[:, 0, r:r + 1],
                                accum_out=stats[:, 1, r:r + 1]))
                    elif item[0] == "values":
                        wait_steps(act, turn, ("pe", "values"))
                        done("act", "V", nc.scalar.activation(V[:].rearrange("p c d -> p (c d)"), banks[5][:, 0:T], ACT.Copy))
                    elif item[0] == "attend":
                        bank = tile_done(act, phase, turn, 3)
                        wait_steps(act, turn, ("dve", "y", 1))
                        nc.scalar.activation(gate_na[:], bank[:, 0:T], ACT.Silu).then_inc(s["evacuated"], 1)

            def y_high(act, phase, turn):
                at = 2 if phase == "ysplitA" else 0
                for k in range(0, KT, 4):
                    done("act", f"y_hi{k}", nc.scalar.activation(y_hi[:, k:k + 4, :], y[:, at + k:at + k + 4, :], ACT.Copy))

            def out(act, phase, turn, last=False):
                for k in range(4):
                    if not last or k + LOOKAHEAD < 4:
                        split_hi(act, phase, turn, k + LOOKAHEAD)
                    if phase != "outA" and k % 2:
                        tile = k // 2
                        tile_read(act, phase, turn, tile)
                        wait_steps(act, turn, ("pool", f"added{tile}", True))
                        xs = x[:, bass.ds(2 * turn + tile, 1), :].rearrange("p a t -> p (a t)")
                        done("act", f"square{tile}", nc.scalar.activation(squares[:, tile, :], xs, ACT.Square))

            def ba(act, phase, turn):
                for k in range(2):
                    split_hi(act, phase, turn, k + LOOKAHEAD)
                bank = tile_done(act, phase, turn, 0)
                done("act", "exp_b", nc.scalar.activation(bt[0:64, :], bank[0:64, 0:T], ACT.Exp, scale=-1.0))
                act.wait_ge(s["small_in"], 16 * SMALL_LOADS)
                nc.scalar.activation(bt2[64:128, :], bank[64:128, 0:T], ACT.Identity,
                                     bias=alog_dt[64:128, 1:2]).then_inc(s["evacuated"], 1)
                tile_read(act, phase, turn, 0)
                done("act", "abs", nc.scalar.activation(bgT[64:128, :], bt2[64:128, :], ACT.Abs))
                wait_steps(act, turn, ("act", "abs"))
                done("act", "exp_g", nc.scalar.activation(bt[64:128, :], bgT[64:128, :], ACT.Exp, scale=-1.0))
                wait_steps(act, turn, ("act", "exp_g"))
                done("act", "log1p", nc.scalar.activation(bgT[64:128, :], bt[64:128, :], ACT.Ln, bias=1.0))
                done("act", "rate", nc.scalar.activation(alog_dt[64:128, 2:3], alog_dt[64:128, 0:1], ACT.Exp))
                for n, dst in enumerate((neg_egc, beta_egl, egl)):
                    wait_steps(act, turn, ("pe", f"sums{n}"))
                    done("act", f"table{n}", nc.scalar.activation(dst[:].rearrange("p c d h -> p (c d h)"),
                                                                  banks[3 + n][:, 0:CHUNKS * 2 * DN_V_HEADS], ACT.Exp))

            def dn(act, phase, turn):
                head, _, _, row = heads(phase, turn)
                if head is not None:
                    wait_steps(act, turn, ("pe", "outB", 1), ("dve", "stateA", 1))
                    act.dma_start(S[:], dram["state"][bass.ds(head, 1)].rearrange("a p u e -> p (a u) e"))\
                        .then_inc(s["state_in"], 16)

                def copy(name, dst, src, *others):
                    wait_steps(act, turn, ("pe", name), *others)
                    done("act", name, nc.scalar.activation(dst, src, ACT.Copy))

                for item in DN_PLANS[phase]:
                    what, arg = item[0], item[1] if len(item) > 1 else None
                    if what == "part" and item[2] == 0:
                        split_hi(act, phase, turn, arg + LOOKAHEAD)
                        if arg in (2, 4, 6, 8):
                            j = arg // 2 - 1
                            bank = tile_done(act, phase, turn, j)
                            wait_steps(act, turn, ("dve", f"conv{(j + 2) % 4}", j < 2))
                            nc.scalar.activation(padded[:, j % 2, PAD:PAD + CTX], bank[:, 0:CTX], ACT.Copy)
                            nc.scalar.activation(padded[:, j % 2, LAT_AT:LAT_AT + LAT], bank[:, CTX:T], ACT.Copy)\
                                .then_inc(s["evacuated"], 1)
                    if what == "part" and item[2] == 3 and arg in (5, 7, 9, 11):
                        j = arg // 2 - 2
                        wait_steps(act, turn, ("dve", f"conv{j}"))
                        i = nc.scalar.activation(conv[:, j, :], conv[:, j, :], ACT.Silu)
                        done("act", f"conv{j}", i)
                    if what == "part" and item[2] == FILL // 2 and arg == 10:
                        bank = tile_done(act, phase, turn, 4)
                        act.wait_ge(s["x_out"], 32 if phase == "dn1" else 16)
                        nc.scalar.activation(y_row(row), bank[:, 0:T], ACT.Silu).then_inc(s["evacuated"], 1)
                    if what == "decay":
                        wait_steps(act, turn, ("pe", f"decay{arg}"), ("pe", "outB", 1))
                        done("act", f"decay{arg}", nc.scalar.activation(decay[arg][:].rearrange("p u i -> p (u i)"),
                                                                        ring(f"decay{arg}")[:], ACT.Exp))
                    elif what == "broad":
                        wait_steps(act, turn, ("pe", f"broad{arg}"))
                        done("act", f"broad{arg}", nc.scalar.activation(q_dec[arg][:].rearrange("p u i -> p (u i)"),
                                                                        ring(f"broad{arg}")[:], ACT.Exp))
                    elif what == "norms":
                        for n in range(2):
                            wait_steps(act, turn, ("pe", f"ss{n}"))
                            done("act", f"ss{n}", nc.scalar.activation(qk_rs[:, n, :], ring(f"ss{n}")[:, 0:CONV_OUT],
                                                                       ACT.Ln, bias=bias_eps[:, 0:1]))
                        for n in range(2):
                            wait_steps(act, turn, ("act", f"ss{n}"))
                            extra = {"bias": bias_eps[:, 1:2]} if n == 0 else {}
                            done("act", f"rs{n}", nc.scalar.activation(qk_rs[:, n, :], qk_rs[:, n, :], ACT.Exp,
                                                                       scale=-0.5, **extra))
                    elif what == "gram":
                        c = arg
                        wait_steps(act, turn, ("pe", f"gram{c}"), ("dve", f"gram{c}"), ("pe", "stateA", True),
                                   ("pe", "state0", True))
                        done("act", f"gram{c}", nc.scalar.activation(k_nat[:, c, :], ring(f"gram{c}")[:, 2 * P:3 * P],
                                                                     ACT.Copy))
                    elif what == "values":
                        copy(f"values{arg}", dn_v[:, :, arg, :],
                             ring(f"values{arg}")[:, 0:T].rearrange("p (c e) -> p c e", c=CHUNKS),
                             ("dve", "recallB", True), ("pe", "apply0", True))
                    elif what == "invert":
                        c = item[2]
                        for name in INVERT[arg]:
                            if name in READ_BY_SCALAR:
                                slot = {"p2": "f", "p2t": "g", "p4": "d", "p4t": "e", "p8t": "f"}.get(
                                    name, "g" if name.startswith("xt") else "x")
                                others = []
                                if name == "xt0":
                                    others = [("dve", f"x1_{c}")]
                                elif name == "p4":
                                    others = [("pool", f"x0{c}")]
                                elif name.startswith("xn"):
                                    others = [("pe", f"xt{name[2:]}_{c}")]
                                copy(f"{name}_{c}", inv[slot, c][:].rearrange("p u i -> p (u i)"),
                                     ring(f"{name}_{c}")[:], *others)
                        if arg == 1:
                            wait_steps(act, turn, ("dve", f"ct_{c}"), ("pool", f"near{c}"))
                            done("act", f"mtr{c}", nc.scalar.activation(inv["mtr", c][:], inv["mt", c][:], ACT.Copy))
                    elif what == "apply":
                        wait_steps(act, turn, ("pe", f"apply{arg}"))
                        for u in range(4):
                            c, d = SCAN[arg][u // 2], u // 2
                            i = nc.scalar.activation(vn[arg][:, u, :], ring(f"apply{arg}")[:, u * P:(u + 1) * P],
                                                     ACT.Copy, scale=beta_now[:, c, d, u % 2:u % 2 + 1])
                        done("act", f"v_new{arg}", i)
                    elif what == "state" and arg == "0":
                        copy("state0", s_out[:].rearrange("p u e -> p (u e)"), ring("state0")[:])
                        wait_steps(act, turn, ("act", "state0"))
                        act.dma_start(dram["state_out"][bass.ds(head, 1)].rearrange("a p u e -> p (a u) e"), s_out[:])\
                            .then_inc(s["state_out"], 16)
                    elif what == "out_norm":
                        wait_steps(act, turn, ("pe", "outB"))
                        for v in range(2):
                            done("act", f"o_sq{v}", nc.scalar.activation(o_sq[:, v, :], banks[6 + v][:, 0:T], ACT.Square))
                        for v in range(2):
                            wait_steps(act, turn, ("pe", f"on{v}"))
                            done("act", f"on{v}", nc.scalar.activation(o_rs[:, v, :], ring(f"on{v}")[:, 0:T], ACT.Ln,
                                                                       bias=bias_eps[:, 0:1], scale=1.0 / P))
                        for v in range(2):
                            wait_steps(act, turn, ("act", f"on{v}"))
                            done("act", f"o_rs{v}", nc.scalar.activation(o_rs[:, v, :], o_rs[:, v, :], ACT.Exp, scale=-0.5))
                        act.wait_ge(s["state_out"], 16 * (head + 1))
                    elif what == "gates":
                        bank = tile_done(act, phase, turn, 5)
                        nc.scalar.activation(y_row(row + 1), bank[:, 0:T], ACT.Silu).then_inc(s["evacuated"], 1)

            def final(act, phase, turn):
                for k in range(KT):
                    wait_steps(act, turn, ("dve", f"final{k}"))
                    act.dma_start(dram["y_out"][:, k, :], x[:, k, :]).then_inc(s["y_out"], 16)
                act.wait_ge(s["y_out"], 16 * KT)
                act.wait_ge(s["k_out"], 16 * NA_HEADS)
                act.wait_ge(s["v_out"], 16 * NA_HEADS)
                act.wait_ge(s["state_out"], 16 * DN_K_HEADS)

            run(act, "act", {"start": start, "squares0": squares_of_x, "norm0": norm, "mod0": modulate, "na": na, "ysplit0": y_high, "out0": out,
                             "norm1": norm, "mod1": modulate, "ba": ba, "dnP": dn,
                             "dn0": dn, "ysplitA": y_high, "outA": out, "dn1": dn, "dnE": dn,
                             "ysplitB": y_high, "outB": out, "norm2": norm, "final": final})

        @block.vector
        def _(dve):
            dve.sem_inc(s["vector_steps"], CREDIT)
            for n in range(RAW_SLOTS):
                dve.sem_inc(consumed[n], 1)

            def start(dve, phase, turn):
                nc.vector.memset(bias_eps[:, 0:1], EPS)
                done("dve", "consts", nc.vector.memset(bias_eps[:, 1:2], float(np.log(SCALE))))
                dve.wait_ge(s["small_in"], 16 * SMALL_LOADS)
                done("dve", "twice", nc.vector.tensor_scalar(twice[:], K["ident"], 2.0, None, ALU.mult))

            def ada_half(turn, k, weights, sums, half):
                for g in range(2):
                    if g == 1:
                        done("dve", f"terms{k}", i)
                        wait_steps(dve, turn, ("dve", f"terms{k}"))
                    i = nc.vector.scalar_tensor_tensor(ada_terms[:], weights, 1.0,
                                                       cond_rows[:, g, half * HALF:(half + 1) * HALF], ALU.mult, ALU.mult,
                                                       accum_out=sums[:, half, g:g + 1])
                return i

            def ada(dve, phase, turn):
                for g in range(ADA_GROUPS):
                    before = None
                    for k, (engine, tile, half) in enumerate(ADA_HALVES):
                        if engine == "dve":
                            if before is not None:
                                half_used(dve, phase, turn, before)
                            before = 16 * g + k
                            slot = raw_wait(dve, phase, turn, before)
                            ada_half(turn, before, raw[:, slot, :], ada_sums[:, g, tile], half).then_inc(consumed[slot], 1)
                    half_used(dve, phase, turn, before)
                    at, n = turn * (8 * ADA_GROUPS) + 8 * g, ADA_TILES["dve"]
                    add_bias(turn, at, n, ada_sums[:, g, :, 0, :], ada_sums[:, g, :, 1, :], f"halves{g}")
                    done("dve", f"mods{g}", nc.vector.tensor_tensor(
                        mods[:, bass.ds(at + n, 3), :], banks[4 + g][:, 0:6].rearrange("p (a b) -> p a b", b=2),
                        ada_b[:, bass.ds(at + n, 3)].unsqueeze(2).broadcast_to([P, 3, 2]), ALU.add))

            def add_bias(turn, at, n, first, second, name):
                done("dve", name, nc.vector.tensor_tensor(mods[:, bass.ds(at, n), :], first, second, ALU.add))
                wait_steps(dve, turn, ("dve", name))
                nc.vector.tensor_tensor(mods[:, bass.ds(at, n), :], mods[:, bass.ds(at, n), :],
                                        ada_b[:, bass.ds(at, n)].unsqueeze(2).broadcast_to([P, n, 2]), ALU.add)

            def low(turn, k):
                if k % 2:
                    wait_steps(dve, turn, ("act", f"shifted{k}"))
                    done("dve", f"hi{k}", nc.vector.tensor_copy(h_hi[:, k, :], shifted[:, k % 2, :]))
                wait_steps(dve, turn, ("dve" if k % 2 else "act", f"hi{k}"))
                done("dve", f"lo{k}", nc.vector.tensor_tensor(h_lo[:, k, :], shifted[:, k % 2, :],
                                                              h_hi[:, k, :].bitcast(F32), ALU.subtract))

            def modulate(dve, phase, turn):
                layer = 0 if phase == "mod0" else 1
                at = layer * 3 * KT + KT
                done("dve", "one", nc.vector.tensor_scalar(gain[:], mods[:, at:at + KT, :], 1.0, None, ALU.add))
                wait_steps(dve, turn, ("dve", "one"))
                done("dve", "gain", nc.vector.tensor_tensor(
                    gain[:], gain[:], norm_w[:, layer, :].unsqueeze(2).broadcast_to([P, KT, 2]), ALU.mult))
                if phase == "mod0":
                    for k in range(LOOKAHEAD):
                        split_lo(dve, "na", 0, k)
                for k in range(KT):
                    if k % 2 == 0:
                        if k >= 2:
                            wait_steps(dve, turn, ("act", f"shifted{k - 2}"))
                        done("dve", f"scaled{k}", nc.vector.tensor_tensor(scaled[:, 0, :], x[:, k, :], rstd[:], ALU.mult))
                    if k >= 1:
                        low(turn, k - 1)
                low(turn, KT - 1)

            def na(dve, phase, turn):
                for item in NA_PLAN:
                    if item[0] == "part" and item[2] == 0:
                        split_lo(dve, phase, turn, item[1] + LOOKAHEAD)
                    elif item[0] == "scores":
                        for r in range(3):
                            wait_steps(dve, turn, ("pe", f"scores{r}"))
                            if r:
                                local = banks[2 + r][:, 0:LAT]
                                done("dve", f"biased{r}", nc.vector.tensor_tensor(
                                    local, local, bias[:, r - 1, bass.ds(turn, 1), :].rearrange("p a k -> p (a k)"), ALU.add))
                                wait_steps(dve, turn, ("dve", f"biased{r}"))
                            else:
                                wait_steps(dve, turn, ("pool", "probs2", 1))
                            wide = slice(0, CTX) if r == 0 else slice(0, T)
                            done("dve", f"max{r}", nc.vector.tensor_reduce(stats[:, 0, r:r + 1], banks[2 + r][:, wide],
                                                                           AX_X, ALU.max, negate=True))
                        for r in range(3):
                            wait_steps(dve, turn, ("act", f"exp{r}"))
                            done("dve", f"rsum{r}", nc.vector.reciprocal(stats[:, 2, r:r + 1], stats[:, 1, r:r + 1]))
                    elif item[0] == "turn_probs":
                        for n in range(2):
                            wait_steps(dve, turn, ("pe", f"probsT{n}"), ("pe", "attend", True))
                            dst = probsT[:, 0:CTX + LAT] if n == 0 else probsT[:, CTX + LAT:CTX + 3 * LAT]
                            src = banks[6][:, 0:CTX + LAT] if n == 0 else banks[2][:]
                            done("dve", f"probsT{n}", nc.vector.tensor_copy(dst, src))
                    elif item[0] == "attend":
                        wait_steps(dve, turn, ("pe", "attend"))
                        tile_read(dve, phase, turn, 3)
                        done("dve", "y", nc.vector.tensor_tensor(
                            y_row(turn), banks[3][:, 0:T], gate_na[:], ALU.mult))
                    elif item[0] == "ada":
                        k = item[1]
                        dve.wait_ge(ada_full[k % 2], 16 * (4 * turn + k // 2 + 1))
                        if k:
                            dve.wait_ge(ada_used[(k - 1) % 2], 4 * turn + (k - 1) // 2 + 2)
                        ada_half(turn, k, raw_ada[:, k % 2, :], ada_sums[:, 0, k // 2], k % 2).then_inc(ada_used[k % 2], 1)
                for slot in range(2):
                    dve.wait_ge(ada_used[slot], 4 * turn + 5)
                sums = ada_sums[:, 0, 0:LATE_TILES]
                add_bias(turn, LATE_TILES * turn + 2 * KT, LATE_TILES, sums[:, :, 0, :], sums[:, :, 1, :], "halves")

            def y_low(dve, phase, turn):
                at = 2 if phase == "ysplitA" else 0
                for k in range(0, KT, 4):
                    wait_steps(dve, turn, ("act", f"y_hi{k}"))
                    done("dve", f"y_lo{k}", nc.vector.tensor_tensor(y_lo[:, k:k + 4, :], y[:, at + k:at + k + 4, :],
                                                                    y_hi[:, k:k + 4, :].bitcast(F32), ALU.subtract))

            def out(dve, phase, turn, last=False):
                layer = 0 if phase == "out0" else 1
                dve.wait_ge(s["x_in"], {"out0": 16, "outA": 32, "outB": 48}[phase])
                for k in range(4):
                    if not last or k + LOOKAHEAD < 4:
                        split_lo(dve, phase, turn, k + LOOKAHEAD)
                    if k % 2:
                        tile = k // 2
                        bank = tile_done(dve, phase, turn, tile)
                        m = 2 * turn + tile
                        for g, sl in ((0, slice(0, CTX)), (1, slice(CTX, T))):
                            xs = x[:, bass.ds(m, 1), sl].rearrange("p a t -> p (a t)")
                            gate = mods[:, bass.ds(m + (layer * 3 + 2) * KT, 1), g:g + 1].rearrange("p a b -> p (a b)")
                            i = nc.vector.scalar_tensor_tensor(xs, bank[:, sl], gate, xs, ALU.mult, ALU.add)
                        i.then_inc(s["evacuated"], 1)

            def ba(dve, phase, turn):
                for k in range(2):
                    split_lo(dve, phase, turn, k + LOOKAHEAD)
                wait_steps(dve, turn, ("act", "exp_b"))
                done("dve", "plus", nc.vector.tensor_scalar(bt[0:64, :], bt[0:64, :], 1.0, None, ALU.add))
                wait_steps(dve, turn, ("dve", "plus"))
                done("dve", "beta", nc.vector.reciprocal(bgT[0:64, :], bt[0:64, :]))
                wait_steps(dve, turn, ("act", "rate"))
                done("dve", "softplus", nc.vector.scalar_tensor_tensor(bt[64:128, :], bt2[64:128, :], 0.0, bgT[64:128, :],
                                                                       ALU.max, ALU.add))
                wait_steps(dve, turn, ("dve", "softplus"))
                done("dve", "g", nc.vector.tensor_scalar(bgT[64:128, :], bt[64:128, :], alog_dt[64:128, 2:3], -1.0,
                                                         ALU.mult, ALU.mult))
                wait_steps(dve, turn, ("pe", "bg"))
                done("dve", "bg", nc.vector.tensor_copy(bg[:].rearrange("p c h -> p (c h)"), banks[2][:, 0:T]))
                wait_steps(dve, turn, ("act", "table1"), ("dve", "bg"))
                done("dve", "neg_egc", nc.vector.tensor_scalar(neg_egc[:], neg_egc[:], -1.0, None, ALU.mult))
                done("dve", "beta_egl", nc.vector.tensor_tensor(
                    beta_egl[:].rearrange("p c d h -> p c (d h)"), beta_egl[:].rearrange("p c d h -> p c (d h)"),
                    bg[:, :, 0:64], ALU.mult))

            def pads(dve, phase, turn):
                nc.vector.memset(padded[:, :, 0:PAD], 0.0)
                nc.vector.memset(padded[:, :, PAD + CTX:LAT_AT], 0.0)
                done("dve", "pads", nc.vector.memset(padded[:, :, LAT_AT + LAT:PADDED], 0.0))

            def dn(dve, phase, turn):
                head, next_head, _, _ = heads(phase, turn)

                def table(t, c, d, v):
                    return t[:, c, d, bass.ds(2 * head + v, 1)]

                if head is not None:
                    wait_steps(dve, turn, ("act", "v_newB", 1))
                    done("dve", "beta_now", nc.vector.tensor_copy(
                        beta_now[:], bg[:, :, 0:64].rearrange("p c (d h) -> p c d h", d=2)[:, :, :, bass.ds(2 * head, 2)]))

                for item in DN_PLANS[phase]:
                    what, arg = item[0], item[1] if len(item) > 1 else None
                    if what == "part" and item[2] == 0:
                        split_lo(dve, phase, turn, arg + LOOKAHEAD)
                    elif what == "squares" and next_head is not None:
                        wait_steps(dve, turn, ("pool", "g_mask2", True))
                        done("dve", "g_now", nc.vector.tensor_copy(
                            g_now[:], bg[:, :, 64:P].rearrange("p c (d h) -> p c d h", d=2)[:, :, :,
                                                                                           bass.ds(2 * next_head, 2)]))
                    at = FILL * arg + item[2] - TAPS_AT if what == "part" else -1
                    if at >= 0 and at % 2 == 0 and at % (2 * FILL) < 2 * CONV and at < 4 * 2 * FILL:
                        j, t = at // (2 * FILL), at % (2 * FILL) // 2
                        if t == 0:
                            tile_read(dve, phase, turn, j)
                            if j < 2:
                                wait_steps(dve, turn, ("pool", f"square{j}", True), ("dve", f"unit{j}"))
                            else:
                                wait_steps(dve, turn, ("pe", f"values{j - 2}"))
                        else:
                            wait_steps(dve, turn, ("dve", f"tap{j}{t - 1}"))
                        w = conv_w[:, bass.ds(next_head, 1), j, t:t + 1].rearrange("p a b -> p (a b)")
                        src = padded[:, j % 2, t:t + CONV_OUT]
                        dst = conv[:, j, :]
                        if t == 0:
                            i = nc.vector.tensor_scalar(dst, src, w, None, ALU.mult)
                        else:
                            i = nc.vector.scalar_tensor_tensor(dst, src, w, dst, ALU.mult, ALU.add)
                        done("dve", f"tap{j}{t}" if t < CONV - 1 else f"conv{j}", i)
                    if what == "unit":
                        for n in range(2):
                            wait_steps(dve, turn, ("act", f"rs{n}"), ("pe", "recallB", True), ("pool", "q_dec2", True))
                            nc.vector.tensor_tensor(dn_qk[:, n, 0:CTX], conv[:, n, 0:CTX], qk_rs[:, n, 0:CTX], ALU.mult)
                            done("dve", f"unit{n}", nc.vector.tensor_tensor(
                                dn_qk[:, n, CTX:T], conv[:, n, CTX + PAD:CONV_OUT], qk_rs[:, n, CTX + PAD:CONV_OUT], ALU.mult))
                    elif what == "gram":
                        c = arg
                        wait_steps(dve, turn, ("pe", f"gram{c}"), ("dve", f"masked{c - 1}") if c else ("dve", "unit1"))
                        both = ring(f"gram{c}")[:, 0:2 * P].rearrange("p (n i) -> p n i", n=2)
                        done("dve", f"gram{c}", nc.vector.tensor_tensor(
                            gram[:], both.unsqueeze(2).broadcast_to([P, 2, 2, P]),
                            consts[:, CONSTS.index("lt"):CONSTS.index("lt") + 4, :]
                            .rearrange("p (n d) i -> p n d i", n=2), ALU.mult))
                        wait_steps(dve, turn, ("dve", f"gram{c}"), ("act", f"decay{c}"), ("pe", f"broad{max(c, 1)}"),
                                   ("pe", "applyB", True))
                        for u in range(4):
                            i = nc.vector.scalar_tensor_tensor(inv["c", c][:, u, :], decay[c][:, u, :],
                                                               beta_now[:, c, u // 2, u % 2:u % 2 + 1],
                                                               gram[:, 0, u // 2, :], ALU.mult, ALU.mult)
                        done("dve", f"c{c}", i)
                        wait_steps(dve, turn, ("dve", f"c{c}"))
                        both = decay[c][:].rearrange("p (d v) i -> p d v i", d=2)
                        done("dve", f"masked{c}", nc.vector.tensor_tensor(
                            both, both, gram[:, 1, :, :].unsqueeze(2).broadcast_to([P, 2, 2, P]), ALU.mult))
                    elif what == "invert":
                        invert(dve, turn, arg, item[2])
                    elif what == "recall":
                        wait_steps(dve, turn, ("pe", f"recall{arg}"))
                        for u in range(4):
                            c = SCAN[arg][u // 2]
                            i = nc.vector.scalar_tensor_tensor(R[arg][:, u, :], ring(f"recall{arg}")[:, u * P:(u + 1) * P],
                                                               table(neg_egc, c, u // 2, u % 2), dn_v[:, c, u % 2, :],
                                                               ALU.mult, ALU.add)
                        done("dve", f"recall{arg}", i)
                    elif what == "apply" and arg != "B":
                        wait_steps(dve, turn, ("act", f"v_new{arg}"))
                        for u in range(4):
                            i = nc.vector.tensor_scalar(vs[arg][:, u, :], ring(f"apply{arg}")[:, u * P:(u + 1) * P],
                                                        table(beta_egl, SCAN[arg][u // 2], u // 2, u % 2), None, ALU.mult)
                        done("dve", f"apply{arg}", i)
                    elif what == "state" and arg == "A":
                        wait_steps(dve, turn, ("pe", "stateA"), ("pe", "outA"))
                        for u in range(4):
                            i = nc.vector.scalar_tensor_tensor(S[:, u, :], S[:, u, :],
                                                               table(egl, SCAN["A"][u // 2], u // 2, u % 2),
                                                               ring("stateA")[:, u * P:(u + 1) * P], ALU.mult, ALU.add)
                        done("dve", "stateA", i)
                    elif what == "out_norm":
                        for v in range(2):
                            wait_steps(dve, turn, ("act", f"o_rs{v}"))
                            done("dve", f"o_n{v}", nc.vector.scalar_tensor_tensor(
                                o_n[:, v, :], banks[6 + v][:, 0:T], dn_norm_w[:, 0:1], o_rs[:, v, :], ALU.mult, ALU.mult))

            def invert(dve, turn, stage, c):
                wide = [P, 4, P]
                ident = K["ident"].unsqueeze(1).broadcast_to(wide)
                near = K["near"].unsqueeze(1).broadcast_to(wide)
                two = twice[:].unsqueeze(1).broadcast_to(wide)

                def psum(name):
                    added = {"x2": [("dve", f"x1_{c}")], "x3": [("dve", f"x2_{c}")]}.get(name, [])
                    wait_steps(dve, turn, ("pe", f"{name}_{c}"), *added, *([("pool", "y1", True)] if name == "ct" else []))
                    return ring(f"{name}_{c}")[:].rearrange("p (u i) -> p u i", u=4)

                if stage == 0:
                    src = psum("ct")
                    done("dve", f"near{c}", nc.vector.tensor_tensor(inv["e", c][:], src, near, ALU.mult))
                    done("dve", f"ct_{c}", nc.vector.tensor_tensor(inv["mt", c][:], src, ident, ALU.add))
                for name in INVERT[stage]:
                    if name in ("x1", "x2", "x3"):
                        src = psum(name)
                        done("dve", f"{name}_{c}", nc.vector.tensor_tensor(inv["x", c][:], src, inv["x", c][:].bitcast(F32),
                                                                          ALU.add))
                    elif name[0] == "t" or name == "res":
                        src = psum(name)
                        done("dve", f"{name}_{c}", nc.vector.scalar_tensor_tensor(
                            inv["d", c][:], src, -1.0, ident if name == "res" else two, ALU.mult, ALU.add))
                    elif name == "xf":
                        src = psum(name)
                        done("dve", f"xf_{c}", nc.vector.tensor_tensor(inv["c", c][:], src, inv["x", c][:].bitcast(F32), ALU.add))

            def final(dve, phase, turn):
                for k in range(KT):
                    done("dve", f"final{k}", nc.vector.scalar_tensor_tensor(x[:, k, :], x[:, k, :], norm_w[:, 2, k:k + 1],
                                                                            rstd[:], ALU.mult, ALU.mult))

            run(dve, "dve", {"start": start, "ada": ada, "mod0": modulate, "na": na, "ysplit0": y_low, "out0": out,
                             "mod1": modulate, "ba": ba, "keep0": pads, "dnP": dn, "dn0": dn,
                             "ysplitA": y_low, "outA": out, "keep1": pads, "dn1": dn, "dnE": dn, "ysplitB": y_low, "outB": out, "final": final})

        @block.gpsimd
        def _(pool):
            pool.sem_inc(s["pool_steps"], CREDIT)

            def lone():
                pool.sem_inc(s["pool_waits"], 1)

            def add(pool, turn, k, n):
                wait_steps(pool, turn, ("act", f"square{n}"))
                done("pool", f"added{n}", nc.gpsimd.tensor_tensor(square_sum, square_sum, squares[:, k, :], ALU.add))

            def squares_of_x(pool, phase, turn):
                done("pool", "zero", nc.gpsimd.memset(square_sum, 0.0))
                wait_steps(pool, turn, ("pool", "zero"))
                for k in range(KT):
                    add(pool, turn, k % 2, k)
                    wait_steps(pool, turn, ("pool", f"added{k}"))
                mask_bias(pool, turn)

            def out(pool, phase, turn, last=False):
                for tile in range(2):
                    wait_steps(pool, turn, ("pool", "added1", True) if tile == 0 else ("pool", "added0"))
                    add(pool, turn, tile, tile)

            def mask_bias(pool, turn):
                pool.wait_ge(s["small_in"], 16 * SMALL_LOADS)
                pool.wait_ge(s["bias_in"], 16 * ROWS * ROWS)
                for r in range(2):
                    grid = K["grid"][:, 0:GRID_W].unsqueeze(1).broadcast_to([P, NA_HEADS * ROWS, GRID_W])
                    b = bias[:, r, :, :].rearrange("p h (i k) -> p (h i) k", i=ROWS)
                    done("pool", f"masked{r}", nc.gpsimd.tensor_tensor(b, b, grid, ALU.add))

            def modulate(pool, phase, turn):
                for k in range(1, KT, 2):
                    if k >= 2:
                        wait_steps(pool, turn, ("act", f"shifted{k - 2}"))
                    done("pool", f"scaled{k}", nc.gpsimd.tensor_tensor(scaled[:, 1, :], x[:, k, :], rstd[:], ALU.mult))

            def na(pool, phase, turn):
                def load_ada(k):
                    pool.wait_ge(ada_used[k % 2], 4 * turn + k // 2 + 1)
                    lone()
                    pool.dma_start(raw_ada[:, k % 2, :],
                                   dram["late"][bass.ds(8 * turn + k, 1)].rearrange("a p f -> p (a f)"))\
                        .then_inc(ada_full[k % 2], 16)

                load_ada(0)
                load_ada(1)
                for cached, name, last in ((cache_k1, "cache_k", "scores2"), (cache_v1, "cache_v", "attend")):
                    wait_steps(pool, turn, ("pe", last, True))
                    lone()
                    pool.dma_start(cached[:], dram[name][bass.ds(turn, 1)].rearrange("a p k -> p (a k)"))\
                        .then_inc(s[f"{name}_in"], 16)
                for item in NA_PLAN:
                    if item[0] == "ada" and item[1] < 6:
                        load_ada(item[1] + 2)
                    elif item[0] == "scores":
                        tile_read(pool, phase, turn, 1)
                        lone()
                        pool.dma_start(dram["k_out"][bass.ds(turn, 1)].rearrange("a p t -> p (a t)"), qk[:, 1, 0:CTX])\
                            .then_inc(s["k_out"], 16)
                        for r in range(3):
                            wait_steps(pool, turn, ("dve", f"rsum{r}"))
                            lone()
                            p = probs[:, 0:CTX] if r == 0 else probs[:, CTX + (r - 1) * T:CTX + r * T]
                            done("pool", f"probs{r}", nc.gpsimd.tensor_scalar(p, p, stats[:, 2, r:r + 1], 1.0,
                                                                              ALU.mult, ALU.mult))
                    elif item[0] == "values":
                        tile_read(pool, phase, turn, 2)
                        lone()
                        pool.dma_start(dram["v_out"][bass.ds(turn, 1)].rearrange("a p t -> p (a t)"), vT[:, 0:CTX])\
                            .then_inc(s["v_out"], 16)
                pool.wait_ge(s["k_out"], 16 * (turn + 1))
                pool.wait_ge(s["v_out"], 16 * (turn + 1))

            def fetch(pool, phase, turn):
                if phase != "fetchA":
                    done("pool", "zero", nc.gpsimd.memset(square_sum, 0.0))
                if phase != "fetch0":
                    pool.wait_ge(s["x_out"], 16 if phase == "fetchA" else 32)
                pool.dma_start(x, dram["x"] if phase == "fetch0" else dram["x_kept"]).then_inc(s["x_in"], 16)

            def keep(pool, phase, turn):
                pool.dma_start(dram["x_kept"], x[:]).then_inc(s["x_out"], 16)
                if phase == "keep1":
                    square_qk(pool, turn)
                    mask_steps(pool, turn)

            def square_qk(pool, turn, *which):
                for n in range(2):
                    wait_steps(pool, turn, ("act", f"conv{n}"), *which)
                    done("pool", f"square{n}", nc.gpsimd.tensor_tensor(qk_sq[:, n, :], conv[:, n, :], conv[:, n, :],
                                                                      ALU.mult))

            def mask_steps(pool, turn, *which):
                for c in range(CHUNKS):
                    wait_steps(pool, turn, ("dve", "g_now"), *which)
                    lone()
                    for u in range(4):
                        d, v = u // 2, u % 2
                        i = nc.gpsimd.tensor_scalar(g_mask[c][:, u, :], K["le" if d == 0 else "ge"],
                                                    g_now[:, c, d, v:v + 1], 1.0, ALU.mult, ALU.mult)
                    done("pool", f"g_mask{c}", i)

            def dn(pool, phase, turn):
                head, _, row, _ = heads(phase, turn)
                for item in DN_PLANS[phase]:
                    what, arg = item[0], item[1] if len(item) > 1 else None
                    if what == "squares" and phase != "dnE":
                        square_qk(pool, turn, ("pe", "applyB"))
                        mask_steps(pool, turn, ("pe", "applyB"))
                    elif what == "gram":
                        near = K["near"].unsqueeze(1).broadcast_to([P, 4, P])
                        ident = K["ident"].unsqueeze(1).broadcast_to([P, 4, P])
                        wait_steps(pool, turn, ("dve", f"c{arg}"), ("pool", "y1", True))
                        done("pool", f"near{arg}", nc.gpsimd.tensor_tensor(inv["d", arg][:], inv["c", arg][:], near, ALU.mult))
                        if arg < CHUNKS - 1:
                            continue
                        for c in range(CHUNKS):
                            wait_steps(pool, turn, ("pool", f"near{c}"))
                            done("pool", f"x0{c}", nc.gpsimd.tensor_tensor(inv["x", c][:], ident,
                                                                          inv["d", c][:].bitcast(F32), ALU.subtract))
                        for c in (1, 2):
                            wait_steps(pool, turn, ("act", f"broad{c}"))
                            q = dn_qk[:, 0, c * P:(c + 1) * P].unsqueeze(1).broadcast_to([P, 4, P])
                            done("pool", f"q_dec{c}", nc.gpsimd.tensor_tensor(q_dec[c][:], q_dec[c][:], q, ALU.mult))
                    elif what == "out_norm":
                        for v in range(2):
                            wait_steps(pool, turn, ("dve", f"o_n{v}"))
                            if phase != "dnE":
                                tile_read(pool, phase, turn, -1)
                            done("pool", f"y{v}", nc.gpsimd.tensor_tensor(
                                y_row(row + v), y_row(row + v), o_n[:, v, :], ALU.mult))

            run(pool, "pool", {"squares0": squares_of_x, "out0": out, "outB": out, "mod0": modulate, "na": na, "fetch0": fetch, "mod1": modulate, "keep0": keep,
                               "dnP": dn, "dn0": dn, "fetchA": fetch, "keep1": keep, "dn1": dn, "dnE": dn,
                               "fetchB": fetch})

    return steps



def tiles(w):
    k, c = w.shape
    return w.reshape(k // (HALF_K * P), HALF_K, P, c // P, P).transpose(3, 0, 2, 1, 4).reshape(c // P, -1, P, HALF)


def columns(v):
    return np.moveaxis(v.reshape(v.shape[:-1] + (v.shape[-1] // P, P)), -1, 0)


def layouts(a):
    ada = [tiles(a["ada_w"][layer]) for layer in range(2)]
    turned = [a["ada_w"][layer].T.reshape(3 * KT, P, 2, HALF).transpose(0, 2, 1, 3) for layer in range(2)]
    first = [(turned if e == "dve" else ada)[0][8 * g + t + (0 if e == "dve" else ADA_TILES["dve"]), half]
             for g in range(4) for e, t, half in ADA_HALVES]
    na_in, na_out = tiles(a["na_w_in"][0]), tiles(a["na_w_out"][0])
    dn_in = tiles(a["dn_w_in"][0])
    late = np.concatenate([turned[0][2 * KT:], turned[1]])
    flat = lambda t: t.reshape(-1, P, HALF)
    stream = [np.stack(first)]
    for h in range(NA_HEADS):
        stream += [flat(na_in[[h, KT + h, 2 * KT + h, 3 * KT + h]])]
    stream += [flat(na_out), flat(dn_in[6 * KT:])]
    head = lambda h: flat(dn_in[[h, KT + h, 2 * KT + 2 * h, 2 * KT + 2 * h + 1, 4 * KT + 2 * h, 4 * KT + 2 * h + 1]])
    order = [2 * (GROUP - 1 - k // 2) + k % 2 for k in range(KT)]
    w_out = a["dn_w_out"][0].reshape(2, KT, P, D_MODEL)
    stream += [head(h) for h in range(GROUP + 1)] + [flat(tiles(w_out[0, order].reshape(-1, D_MODEL)))]
    stream += [head(h) for h in range(GROUP + 1, DN_K_HEADS)] + [flat(tiles(w_out[1].reshape(-1, D_MODEL)))]
    x = np.concatenate([a["x_prompt"][0], a["x_sample"][0]])
    rpb = np.zeros((NA_HEADS, 2 * ROWS - 1, BIAS_W), np.float32)
    at = GRID_W - WIN_C
    rpb[:, :, at:at + 2 * WIN_C - 1] = a["na_rpb"][0][:, WIN_R - ROWS:WIN_R + ROWS - 1]
    rpb = np.tile(rpb, (1, 1, GRID_W))
    conv = a["dn_conv_w"][0].reshape(CONV, 4 * KT, P)
    heads = np.array([[h, KT + h, 2 * KT + 2 * h, 2 * KT + 2 * h + 1] for h in range(DN_K_HEADS)])
    state = a["state_dn"][0, 0].reshape(2, DN_K_HEADS, 2, P, P)
    alog_dt = np.zeros((P, 2), np.float32)
    alog_dt[64:, 0] = a["dn_a_log"][0].reshape(-1)
    alog_dt[64:, 1] = a["dn_dt_bias"][0].reshape(-1)
    return {
        "stream": np.concatenate(stream),
        "late": flat(late),
        "consts": shape_constants().reshape(P, len(CONSTS), P),
        "cond": columns(np.stack([a["c_ctx"], a["c"][0]])).transpose(0, 2, 1),
        "ada_b": columns(a["ada_b"]).reshape(P, -1),
        "norm_w": columns(np.concatenate([a["norm_w"], a["final_norm_w"][None]])),
        "x": columns(x).transpose(0, 2, 1),
        "cond_rows": np.stack([a["c_ctx"], a["c"][0]]),
        "cache_k": a["cache_na_k"][0, 0].transpose(1, 2, 0),
        "cache_v": a["cache_na_v"][0, 0].transpose(1, 0, 2),
        "rpb": rpb,
        "conv_w": conv[:, heads].transpose(3, 1, 2, 0),
        "alog_dt": alog_dt,
        "dn_norm_w": a["dn_norm_w"][0][:, None],
        "state": state.transpose(1, 3, 0, 2, 4).reshape(DN_K_HEADS, P, 4, P),
    }


OUTS = {"y_out": (P, KT, T), "k_out": (NA_HEADS, P, CTX), "v_out": (NA_HEADS, P, CTX),
        "state_out": (DN_K_HEADS, P, 4, P)}


def build(nc, shapes):
    def declare(nc):
        dram = {n: nc.dram_tensor(f"in_{n}", shape, F32, kind="ExternalInput").ap() for n, shape in shapes.items()}
        dram |= {n: nc.dram_tensor(f"out_{n}", shape, F32, kind="ExternalOutput").ap() for n, shape in OUTS.items()}
        dram["x_kept"] = nc.dram_tensor("x_kept", (P, KT, T), F32).ap()
        return dram
    listed = type(nc)("TRN2", target_bir_lowering=False, num_devices=1)
    known = emit(listed, None, declare(listed))
    emit(nc, known, declare(nc))


def kernel(**inputs):
    import concourse.bacc as bacc
    from concourse.bass_utils import run_bass_kernel_spmd

    arrays = {n: np.ascontiguousarray(v) for n, v in layouts({k: np.asarray(v) for k, v in inputs.items()}).items()}
    nc = bacc.Bacc("TRN2", target_bir_lowering=False, num_devices=1)
    build(nc, {n: v.shape for n, v in arrays.items()})
    got = run_bass_kernel_spmd(nc, [{f"in_{n}": v for n, v in arrays.items()}], core_ids=[0]).results[0]
    y = got["out_y_out"].transpose(2, 1, 0).reshape(T, D_MODEL)
    state = got["out_state_out"].reshape(DN_K_HEADS, P, 2, 2, P).transpose(2, 0, 3, 1, 4)
    return (np.ascontiguousarray(y[None, :CTX]), np.ascontiguousarray(y[None, CTX:]),
            np.ascontiguousarray(got["out_k_out"].transpose(2, 0, 1)[None, None]),
            np.ascontiguousarray(got["out_v_out"].transpose(2, 0, 1)[None, None]),
            np.ascontiguousarray(state.reshape(1, 1, 2, DN_V_HEADS, P, P)))
```
